# Optimizing a Trainium2 kernel written in Bass

```python
import jax, jax.numpy as jnp
from jax import lax
import numpy as np
import math

D_MODEL = 1024
BATCH = 1
SEQ = 256
DEPTH = 2

CHUNK = 64
N_MIXERS = 2
ROPE_THETA = 500000.0
EPS = 1e-6

A_HEADS = 16
A_KV_HEADS = 4
A_HEAD_DIM = 64
A_ROT = A_HEAD_DIM // 4
IDX_HEADS = 8
IDX_DIM = 64
IDX_ROT = IDX_DIM // 4
IDX_TOPK_MAX = 256
IDX_WEIGHT_SCALE = (IDX_HEADS ** -0.5) * (IDX_DIM ** -0.5)
A_QBLK = CHUNK
A_IN = A_HEADS * A_HEAD_DIM + 2 * A_KV_HEADS * A_HEAD_DIM + IDX_HEADS * IDX_DIM + IDX_DIM + IDX_HEADS

B_HEADS = 16
B_NOPE = 64
B_ROPE = 32
B_V = 64
B_Q_LORA = 384
B_KV_LORA = 256
B_QBLK = 128
B_IN = B_Q_LORA + B_KV_LORA + B_ROPE

D_FF = 4 * D_MODEL

N_A = (DEPTH + 1) // 2
N_B = DEPTH // 2


def rms_norm(x, g):
    xf = x.astype(jnp.float32)
    y = xf * lax.rsqrt(jnp.mean(xf * xf, axis=-1, keepdims=True) + EPS)
    return (y * g.astype(jnp.float32)).astype(x.dtype)

def rope_angles(positions, rot_dim):
    inv = ROPE_THETA ** (-jnp.arange(0, rot_dim, 2, dtype=jnp.float32) / rot_dim)
    ang = positions.astype(jnp.float32)[..., None] * inv
    return jnp.cos(ang), jnp.sin(ang)

def apply_rope(x, cos, sin):
    half = x.shape[-1] // 2
    x1 = x[..., :half].astype(jnp.float32)
    x2 = x[..., half:].astype(jnp.float32)
    c = cos[:, :, None, :]
    s = sin[:, :, None, :]
    return jnp.concatenate([x1 * c - x2 * s, x2 * c + x1 * s], axis=-1).astype(x.dtype)

def partial_rope(x, cos, sin, rot):
    return jnp.concatenate([apply_rope(x[..., :rot], cos, sin), x[..., rot:]], axis=-1)

def dsa_mixer(h, w_in, w_out, cos_a, sin_a, cos_i, sin_i):
    bsz, seq, _ = h.shape
    f32 = jnp.float32
    n_q = A_HEADS * A_HEAD_DIM
    n_kv = A_KV_HEADS * A_HEAD_DIM
    n_qi = IDX_HEADS * IDX_DIM
    cuts = [n_q, n_q + n_kv, n_q + 2 * n_kv, n_q + 2 * n_kv + n_qi, n_q + 2 * n_kv + n_qi + IDX_DIM]
    proj = h @ w_in
    q, k, v, qi, ki, wi = jnp.split(proj, cuts, axis=-1)
    q = partial_rope(q.reshape(bsz, seq, A_HEADS, A_HEAD_DIM), cos_a, sin_a, A_ROT)
    k = partial_rope(k.reshape(bsz, seq, A_KV_HEADS, A_HEAD_DIM), cos_a, sin_a, A_ROT)
    v = v.reshape(bsz, seq, A_KV_HEADS, A_HEAD_DIM)
    qi = partial_rope(qi.reshape(bsz, seq, IDX_HEADS, IDX_DIM), cos_i, sin_i, IDX_ROT)
    ki = partial_rope(ki[:, :, None, :], cos_i, sin_i, IDX_ROT)[:, :, 0, :]
    wi = wi.astype(f32) * IDX_WEIGHT_SCALE

    top_k = min(IDX_TOPK_MAX, seq // 4)
    group = A_HEADS // A_KV_HEADS
    scale = A_HEAD_DIM ** -0.5
    key_pos = jnp.arange(seq)

    def block(i):
        start = i * A_QBLK
        qb = lax.dynamic_slice_in_dim(q, start, A_QBLK, axis=1)
        qib = lax.dynamic_slice_in_dim(qi, start, A_QBLK, axis=1)
        wib = lax.dynamic_slice_in_dim(wi, start, A_QBLK, axis=1)
        q_pos = start + jnp.arange(A_QBLK)
        chunk_end = (q_pos // CHUNK + 1) * CHUNK
        logits = jnp.einsum('bthd,bsd->bths', qib, ki, preferred_element_type=f32)
        score = jnp.einsum('bths,bth->bts', jax.nn.relu(logits), wib)
        visible = key_pos[None, :] < chunk_end[:, None]
        score = jnp.where(visible[None], score, -jnp.inf)
        _, sel = lax.top_k(score, top_k)
        sel_ok = sel < chunk_end[None, :, None]
        flat = sel.reshape(bsz, A_QBLK * top_k)[:, :, None, None]
        kg = jnp.take_along_axis(k, flat, axis=1).reshape(bsz, A_QBLK, top_k, A_KV_HEADS, A_HEAD_DIM)
        vg = jnp.take_along_axis(v, flat, axis=1).reshape(bsz, A_QBLK, top_k, A_KV_HEADS, A_HEAD_DIM)
        qg = qb.reshape(bsz, A_QBLK, A_KV_HEADS, group, A_HEAD_DIM)
        s = jnp.einsum('btgrd,btkgd->btgrk', qg, kg, preferred_element_type=f32) * scale
        s = jnp.where(sel_ok[:, :, None, None, :], s, -jnp.inf)
        p = jax.nn.softmax(s, axis=-1)
        o = jnp.einsum('btgrk,btkgd->btgrd', p.astype(vg.dtype), vg, preferred_element_type=f32)
        return o.reshape(bsz, A_QBLK, A_HEADS * A_HEAD_DIM).astype(h.dtype)

    o = lax.map(block, jnp.arange(seq // A_QBLK))
    o = jnp.moveaxis(o, 0, 1).reshape(bsz, seq, A_HEADS * A_HEAD_DIM)
    return o @ w_out

def mla_mixer(h, w_in, q_norm, kv_norm, w_q_up, w_kv_up, w_out, cos_b, sin_b):
    bsz, seq, _ = h.shape
    f32 = jnp.float32
    proj = h @ w_in
    cq, ckv, kr = jnp.split(proj, [B_Q_LORA, B_Q_LORA + B_KV_LORA], axis=-1)
    cq = rms_norm(cq, q_norm)
    ckv = rms_norm(ckv, kv_norm)
    qf = (cq @ w_q_up).reshape(bsz, seq, B_HEADS, B_NOPE + B_ROPE)
    q_nope, q_rope = qf[..., :B_NOPE], apply_rope(qf[..., B_NOPE:], cos_b, sin_b)
    kr = apply_rope(kr[:, :, None, :], cos_b, sin_b)[:, :, 0, :]
    kv = (ckv @ w_kv_up).reshape(bsz, seq, B_HEADS, B_NOPE + B_V)
    k_nope, v = kv[..., :B_NOPE], kv[..., B_NOPE:]
    scale = (B_NOPE + B_ROPE) ** -0.5
    key_pos = jnp.arange(seq)

    def block(i):
        start = i * B_QBLK
        qn = lax.dynamic_slice_in_dim(q_nope, start, B_QBLK, axis=1)
        qr = lax.dynamic_slice_in_dim(q_rope, start, B_QBLK, axis=1)
        s = (jnp.einsum('bthd,bshd->bhts', qn, k_nope, preferred_element_type=f32)
             + jnp.einsum('bthd,bsd->bhts', qr, kr, preferred_element_type=f32)) * scale
        q_pos = start + jnp.arange(B_QBLK)
        chunk_end = (q_pos // CHUNK + 1) * CHUNK
        mask = key_pos[None, :] < chunk_end[:, None]
        s = jnp.where(mask[None, None], s, -jnp.inf)
        p = jax.nn.softmax(s, axis=-1)
        o = jnp.einsum('bhts,bshd->bthd', p.astype(v.dtype), v, preferred_element_type=f32)
        return o.reshape(bsz, B_QBLK, B_HEADS * B_V).astype(h.dtype)

    o = lax.map(block, jnp.arange(seq // B_QBLK))
    o = jnp.moveaxis(o, 0, 1).reshape(bsz, seq, B_HEADS * B_V)
    return o @ w_out

def squared_relu_mlp(h, w_up, w_down):
    a = jax.nn.relu(h @ w_up)
    return (a * a) @ w_down

def first_inputs(seed: int = 0) -> dict:
    key = jax.random.key(seed)
    ks = jax.random.split(key, 20)
    f32 = jnp.float32

    def nrm(k, shape, fan_in):
        return jax.random.normal(k, shape, f32) * (fan_in ** -0.5)

    def gain(k, shape):
        return 1.0 + 0.02 * jax.random.normal(k, shape, f32)

    x = jax.random.normal(ks[0], (BATCH, SEQ, D_MODEL), f32)
    starts = jax.random.randint(ks[1], (BATCH, 1), 0, 64, dtype=jnp.int32) * CHUNK
    positions = (starts + jnp.arange(SEQ, dtype=jnp.int32)[None, :]).astype(jnp.int32)
    return {
        'x': x,
        'positions': positions,
        'attn_norm': gain(ks[2], (DEPTH, D_MODEL)),
        'mlp_norm': gain(ks[3], (DEPTH, D_MODEL)),
        'a_w_in': nrm(ks[4], (N_A, D_MODEL, A_IN), D_MODEL),
        'a_w_out': nrm(ks[5], (N_A, A_HEADS * A_HEAD_DIM, D_MODEL), A_HEADS * A_HEAD_DIM),
        'b_w_in': nrm(ks[6], (N_B, D_MODEL, B_IN), D_MODEL),
        'b_q_norm': gain(ks[7], (N_B, B_Q_LORA)),
        'b_kv_norm': gain(ks[8], (N_B, B_KV_LORA)),
        'b_w_q_up': nrm(ks[9], (N_B, B_Q_LORA, B_HEADS * (B_NOPE + B_ROPE)), B_Q_LORA),
        'b_w_kv_up': nrm(ks[10], (N_B, B_KV_LORA, B_HEADS * (B_NOPE + B_V)), B_KV_LORA),
        'b_w_out': nrm(ks[11], (N_B, B_HEADS * B_V, D_MODEL), B_HEADS * B_V),
        'mlp_w_up': nrm(ks[12], (DEPTH, D_MODEL, D_FF), D_MODEL),
        'mlp_w_down': nrm(ks[13], (DEPTH, D_FF, D_MODEL), D_FF),
        'final_norm': gain(ks[14], (D_MODEL,)),
    }

def first_block(x, positions, attn_norm, mlp_norm, a_w_in, a_w_out, b_w_in, b_q_norm, b_kv_norm,
              b_w_q_up, b_w_kv_up, b_w_out, mlp_w_up, mlp_w_down, final_norm):
    cos_a, sin_a = rope_angles(positions, A_ROT)
    cos_i, sin_i = rope_angles(positions, IDX_ROT)
    cos_b, sin_b = rope_angles(positions, B_ROPE)
    for i in range(DEPTH):
        h = rms_norm(x, attn_norm[i])
        j = i // N_MIXERS
        if i % N_MIXERS == 0:
            x = x + dsa_mixer(h, a_w_in[j], a_w_out[j], cos_a, sin_a, cos_i, sin_i)
        else:
            x = x + mla_mixer(h, b_w_in[j], b_q_norm[j], b_kv_norm[j], b_w_q_up[j],
                              b_w_kv_up[j], b_w_out[j], cos_b, sin_b)
        h = rms_norm(x, mlp_norm[i])
        x = x + squared_relu_mlp(h, mlp_w_up[i], mlp_w_down[i])
    return rms_norm(x, final_norm)


N_META = 16
POOL_WINDOWS = (2, 4, 8, 16)
N_POOL_GROUPS = len(POOL_WINDOWS)
POOL_GROUP = D_MODEL // N_POOL_GROUPS
DIFF_HEAD_DIM = 64
DIFF_HEADS = D_MODEL // (2 * DIFF_HEAD_DIM)
D_FF_2 = 256 * ((8 * D_MODEL // 3 + 255) // 256)
Q_BLOCK = 128
N_POOL_LAYERS = (DEPTH + 1) // 2
N_ATTN_LAYERS = DEPTH // 2


def rmsnorm(x, g):
    xf = x.astype(jnp.float32)
    y = xf * lax.rsqrt(jnp.mean(xf * xf, axis=-1, keepdims=True) + EPS)
    return (y * g.astype(jnp.float32)).astype(x.dtype)

def swiglu(h, w1, w3, w2):
    return (jax.nn.silu(h @ w1) * (h @ w3)) @ w2

def lambda_init_fn(layer_idx):
    return 0.8 - 0.6 * math.exp(-0.3 * layer_idx)

def causal_multiscale_pool(h, w, b, scale):
    bsz, L, D = h.shape
    hf = h.astype(jnp.float32)
    cs = jnp.pad(jnp.cumsum(hf, axis=1), ((0, 0), (1, 0), (0, 0)))
    hg = hf.reshape(bsz, L, N_POOL_GROUPS, POOL_GROUP)
    csg = cs.reshape(bsz, L + 1, N_POOL_GROUPS, POOL_GROUP)
    t = jnp.arange(L)
    pooled = []
    for g, win in enumerate(POOL_WINDOWS):
        lo = jnp.maximum(t + 1 - win, 0)
        cnt = (t + 1 - lo).astype(jnp.float32)
        pooled.append((csg[:, 1:, g] - csg[:, lo, g]) / cnt[None, :, None])
    pooled = jnp.stack(pooled, axis=2)
    diff = (pooled - hg).astype(h.dtype)
    y = jnp.einsum('blgc,gcd->blgd', diff, w) + b
    return y.reshape(bsz, L, D) * scale

def diff_attention(h, w_qkv, w_o, lq1, lk1, lq2, lk2, subln_g, lambda_init):
    bsz, L, D = h.shape
    H, d = DIFF_HEADS, DIFF_HEAD_DIM
    q, k, v = jnp.split(h @ w_qkv, 3, axis=-1)
    q = q.reshape(bsz, L, H, 2, d)
    k = k.reshape(bsz, L, H, 2, d)
    v = v.reshape(bsz, L, H, 2 * d)
    lam = (jnp.exp(jnp.sum(lq1.astype(jnp.float32) * lk1.astype(jnp.float32)))
           - jnp.exp(jnp.sum(lq2.astype(jnp.float32) * lk2.astype(jnp.float32)))
           + lambda_init)
    n_blk = -(-L // Q_BLOCK)
    Lp = n_blk * Q_BLOCK
    qb = jnp.pad(q, ((0, 0), (0, Lp - L), (0, 0), (0, 0), (0, 0)))
    qb = qb.reshape(bsz, n_blk, Q_BLOCK, H, 2, d).transpose(1, 0, 2, 3, 4, 5)
    key_pos = jnp.arange(L)
    neg = jnp.finfo(jnp.float32).min

    def block(args):
        qi, i = args
        s = jnp.einsum('bqhcd,bkhcd->bhcqk', qi, k).astype(jnp.float32) * (d ** -0.5)
        qpos = i * Q_BLOCK + jnp.arange(Q_BLOCK)
        mask = key_pos[None, :] <= qpos[:, None]
        p = jax.nn.softmax(jnp.where(mask, s, neg), axis=-1)
        a = p[:, :, 0] - lam * p[:, :, 1]
        return jnp.einsum('bhqk,bkhe->bqhe', a.astype(v.dtype), v)

    o = lax.map(block, (qb, jnp.arange(n_blk)))
    o = o.transpose(1, 0, 2, 3, 4).reshape(bsz, Lp, H, 2 * d)[:, :L]
    o = rmsnorm(o, subln_g) * (1.0 - lambda_init)
    return o.reshape(bsz, L, H * 2 * d) @ w_o

def second_inputs(seed: int = 0) -> dict:
    key = jax.random.key(seed)
    ks = jax.random.split(key, 20)
    f32 = jnp.float32
    nrm = lambda k, s, sc: jax.random.normal(k, s, f32) * sc
    gain = lambda k, s: 1.0 + 0.02 * jax.random.normal(k, s, f32)
    NP, NA = N_POOL_LAYERS, N_ATTN_LAYERS
    return {
        'x': jax.random.normal(ks[0], (BATCH, SEQ, D_MODEL), f32),
        'meta_tokens': nrm(ks[1], (N_META, D_MODEL), 1.0),
        'ffn_norm_pre': gain(ks[2], (DEPTH, 2, D_MODEL)),
        'ffn_norm_post': gain(ks[3], (DEPTH, 2, D_MODEL)),
        'ffn_w1': nrm(ks[4], (DEPTH, 2, D_MODEL, D_FF_2), D_MODEL ** -0.5),
        'ffn_w3': nrm(ks[5], (DEPTH, 2, D_MODEL, D_FF_2), D_MODEL ** -0.5),
        'ffn_w2': nrm(ks[6], (DEPTH, 2, D_FF_2, D_MODEL), D_FF_2 ** -0.5),
        'mix_norm_pre': gain(ks[7], (DEPTH, D_MODEL)),
        'mix_norm_post': gain(ks[8], (DEPTH, D_MODEL)),
        'pool_w': nrm(ks[9], (NP, N_POOL_GROUPS, POOL_GROUP, POOL_GROUP), POOL_GROUP ** -0.5),
        'pool_b': nrm(ks[10], (NP, N_POOL_GROUPS, POOL_GROUP), 0.01),
        'pool_scale': 1.0 + 0.1 * jax.random.normal(ks[11], (NP, D_MODEL), f32),
        'attn_w_qkv': nrm(ks[12], (NA, D_MODEL, 3 * D_MODEL), D_MODEL ** -0.5),
        'attn_w_o': nrm(ks[13], (NA, D_MODEL, D_MODEL), D_MODEL ** -0.5),
        'attn_lambda_q1': nrm(ks[14], (NA, DIFF_HEAD_DIM), 0.1),
        'attn_lambda_k1': nrm(ks[15], (NA, DIFF_HEAD_DIM), 0.1),
        'attn_lambda_q2': nrm(ks[16], (NA, DIFF_HEAD_DIM), 0.1),
        'attn_lambda_k2': nrm(ks[17], (NA, DIFF_HEAD_DIM), 0.1),
        'attn_subln': gain(ks[18], (NA, 2 * DIFF_HEAD_DIM)),
    }

def second_block(x, meta_tokens, ffn_norm_pre, ffn_norm_post, ffn_w1, ffn_w3, ffn_w2,
              mix_norm_pre, mix_norm_post, pool_w, pool_b, pool_scale,
              attn_w_qkv, attn_w_o, attn_lambda_q1, attn_lambda_k1, attn_lambda_q2,
              attn_lambda_k2, attn_subln):
    bsz = x.shape[0]
    meta = jnp.broadcast_to(meta_tokens[None].astype(x.dtype), (bsz, N_META, x.shape[-1]))
    h = jnp.concatenate([meta, x], axis=1)
    for i in range(DEPTH):
        f = swiglu(rmsnorm(h, ffn_norm_pre[i, 0]), ffn_w1[i, 0], ffn_w3[i, 0], ffn_w2[i, 0])
        h = h + 0.5 * rmsnorm(f, ffn_norm_post[i, 0])
        hn = rmsnorm(h, mix_norm_pre[i])
        j = i // N_MIXERS
        if i % N_MIXERS == 0:
            m = causal_multiscale_pool(hn, pool_w[j], pool_b[j], pool_scale[j])
        else:
            m = diff_attention(hn, attn_w_qkv[j], attn_w_o[j], attn_lambda_q1[j],
                               attn_lambda_k1[j], attn_lambda_q2[j], attn_lambda_k2[j],
                               attn_subln[j], lambda_init_fn(i))
        h = h + rmsnorm(m, mix_norm_post[i])
        f = swiglu(rmsnorm(h, ffn_norm_pre[i, 1]), ffn_w1[i, 1], ffn_w3[i, 1], ffn_w2[i, 1])
        h = h + 0.5 * rmsnorm(f, ffn_norm_post[i, 1])
    return h[:, N_META:]


def setup_inputs(seed=0):
    out = dict(first_inputs(seed))
    for name, value in second_inputs(seed + 1).items():
        if name != "x":
            out[name + "_2"] = value
    return out


def reference(
    x, positions, attn_norm, mlp_norm, a_w_in, a_w_out, b_w_in, b_q_norm, b_kv_norm, b_w_q_up,
    b_w_kv_up, b_w_out, mlp_w_up, mlp_w_down, final_norm, meta_tokens_2, ffn_norm_pre_2,
    ffn_norm_post_2, ffn_w1_2, ffn_w3_2, ffn_w2_2, mix_norm_pre_2, mix_norm_post_2, pool_w_2,
    pool_b_2, pool_scale_2, attn_w_qkv_2, attn_w_o_2, attn_lambda_q1_2, attn_lambda_k1_2,
    attn_lambda_q2_2, attn_lambda_k2_2, attn_subln_2,
):
    x = first_block(
        x, positions, attn_norm, mlp_norm, a_w_in, a_w_out, b_w_in, b_q_norm, b_kv_norm,
        b_w_q_up, b_w_kv_up, b_w_out, mlp_w_up, mlp_w_down, final_norm,
    )
    return second_block(
        x, meta_tokens_2, ffn_norm_pre_2, ffn_norm_post_2, ffn_w1_2, ffn_w3_2, ffn_w2_2,
        mix_norm_pre_2, mix_norm_post_2, pool_w_2, pool_b_2, pool_scale_2, attn_w_qkv_2,
        attn_w_o_2, attn_lambda_q1_2, attn_lambda_k1_2, attn_lambda_q2_2, attn_lambda_k2_2,
        attn_subln_2,
    )


_drawn_inputs = setup_inputs


def setup_inputs(seed=0):
    import zlib

    import numpy as np

    out = dict(_drawn_inputs(seed))
    spreads = {}
    factors = {'b_q_norm': 8.0,
     'b_kv_norm': 8.0,
     'ffn_norm_post_2': 3.556,
     'mix_norm_post_2': 2.851,
     'attn_lambda_q1_2': 5.519,
     'attn_lambda_k1_2': 5.336,
     'attn_lambda_q2_2': 7.352,
     'attn_subln_2': 5.179}
    for name, (base, spread) in spreads.items():
        noise = np.random.default_rng([zlib.crc32(name.encode()), seed]).standard_normal(out[name].shape)
        drawn = base * np.exp(spread * noise) if base else spread * noise
        out[name] = __import__('jax').numpy.asarray(drawn.astype(out[name].dtype))
    for name, factor in factors.items():
        out[name] = (out[name] * factor).astype(out[name].dtype)
    return out
```

```python
from contextlib import ExitStack
import math

import numpy as np

import concourse.bass as bass
from concourse import mybir

F32 = mybir.dt.float32
F32R = mybir.dt.float32r
I32 = mybir.dt.int32
ACT = mybir.ActivationFunctionType
ALU = mybir.AluOpType
AX = mybir.AxisListType
ds = bass.ds

P = 128
D = 1024
KD = D // P
SEQ = 256
META = 16
T2 = SEQ + META
CHUNK = 64
TOPK = 64
EPS = 1e-6
THETA = 500000.0

A_HEADS, A_KV, HD = 16, 4, 64
A_ROT = HD // 4
IDX_HEADS = 8
IDX_SCALE = (IDX_HEADS ** -0.5) * (HD ** -0.5)
A_SCALE = HD ** -0.5
Q_COLS, KV_COLS, QI_COLS = A_HEADS * HD, A_KV * HD, IDX_HEADS * HD

B_HEADS, B_NOPE, B_ROPE, B_V = 16, 64, 32, 64
B_QK = B_NOPE + B_ROPE
B_QL, B_KVL = 384, 256
KQL, KKV = B_QL // P, B_KVL // P
B_SCALE = B_QK ** -0.5

D_FF = 4 * D
KF = D_FF // P
D_FF2 = 256 * ((8 * D // 3 + 255) // 256)
KF2 = D_FF2 // P
WINDOWS = (2, 4, 8, 16)
DIFF_HEADS = 8
DIFF_SCALE = HD ** -0.5
LAMBDA_INIT = 0.8 - 0.6 * math.exp(-0.3 * 1)

SLOT = KF2 * P
NEG = -1e30
TAKEN = -3e38

C_ID = 0
C_RA = C_ID + P
C_RB = C_RA + P
C_INVA = C_RB + B_QK
C_INVB = C_INVA + 1
C_CHUNK = C_INVB + 1
C_CAUSAL = C_CHUNK + 2 * SEQ
C_ALL = C_CAUSAL + 2 * T2

VEC_A = [("attn_norm", 2 * KD), ("mlp_norm", 2 * KD), ("final_norm", KD),
         ("ffn_norm_pre_2", 4 * KD), ("ffn_norm_post_2", 4 * KD)]
VEC_B = [("mix_norm_pre_2", 2 * KD), ("mix_norm_post_2", 2 * KD), ("pool_b_2", KD), ("pool_scale_2", KD),
         ("b_q_norm", KQL), ("b_kv_norm", KKV), ("attn_subln_2", 1)]
GAIN = {}
_at = 0
for _name, _rows in VEC_A + VEC_B:
    GAIN[_name] = _at
    _at += _rows
N_VEC_A = sum(r for _, r in VEC_A)
N_VEC_B = sum(r for _, r in VEC_B)

TURN_PARTS = []
_rest = 2 * math.pi
for _bits in (5, 13, 21):
    _part = math.floor(_rest * 2 ** _bits) / 2 ** _bits
    TURN_PARTS.append(_part)
    _rest -= _part
TURN_PARTS.append(_rest)
ROUND = 1.5 * 2 ** 23


def constants():
    c = np.zeros((P, C_ALL), np.float32)
    c[:, C_ID:C_ID + P] = np.eye(P)
    for head in (0, HD):
        for d in range(A_ROT // 2):
            c[head + A_ROT // 2 + d, C_RA + head + d] = -1
            c[head + d, C_RA + head + A_ROT // 2 + d] = 1
    for d in range(B_ROPE // 2):
        c[B_NOPE + B_ROPE // 2 + d, C_RB + B_NOPE + d] = -1
        c[B_NOPE + d, C_RB + B_NOPE + B_ROPE // 2 + d] = 1
    inv_a = np.float32(THETA) ** (-np.arange(0, A_ROT, 2, dtype=np.float32) / A_ROT)
    inv_b = np.float32(THETA) ** (-np.arange(0, B_ROPE, 2, dtype=np.float32) / B_ROPE)
    for head in (0, HD):
        c[head:head + A_ROT, C_INVA] = np.tile(inv_a, 2)
    c[B_NOPE:B_QK, C_INVB] = np.tile(inv_b, 2)
    key = np.arange(T2)[None]
    for i in range(2):
        row = (i * P + np.arange(P))[:, None]
        c[:, C_CHUNK + i * SEQ:C_CHUNK + (i + 1) * SEQ] = np.where(key[:, :SEQ] < (row // CHUNK + 1) * CHUNK, 0, NEG)
        c[:, C_CAUSAL + i * T2:C_CAUSAL + (i + 1) * T2] = np.where(key <= row + META, 0, NEG)
    t = np.arange(T2)
    window = np.stack([1.0 / np.minimum(t + 1, w) for w in WINDOWS]).astype(np.float32)
    return c, window


def at(n, it, per):
    return n if it is None else it * per + n


class Flat:

    def __init__(self, tensor, shift):
        self.tensor, self.shift = tensor, shift

    def __getitem__(self, key):
        p, k, t = key
        return self.tensor[p, k, t.start - self.shift:t.stop - self.shift]


class Counts:

    def __init__(self):
        self.n = {}

    def add(self, name, k=1):
        self.n[name] = self.n.get(name, 0) + k
        return self.n[name]

    def get(self, name):
        return self.n.get(name, 0)


class Gemm:

    def __init__(self, name, sizes, units, reader="dve_evac", dmas=None):
        self.name, self.sizes, self.units, self.reader = name, sizes, units, reader
        self.dmas = dmas or [1] * len(sizes)


def plan():
    def mlp(i):
        return [Gemm(f"mlp_up{i}", [KD * 256] * (KF // 2), KF // 2), Gemm(f"mlp_down{i}", [16 * P] * (KD * 2), KD)]

    def ffn(i):
        return [Gemm(f"ffn_up{i}", [KD * 256] * KF2, KF2), Gemm(f"ffn_down{i}", [KF2 * P] * KD, KD, "act_evac")]

    gemms = [
        Gemm("a_in", [KD * 256] * 2 + [KD * 136] + [KD * 256] * 6, 9, dmas=[1, 1, 3, 4, 4, 4, 4, 1, 1]),
        Gemm("a_out", [KD * 256] * 4, 4), *mlp(0),
        Gemm("b_in", [KD * 256] * 2 + [KD * 160], 3),
        Gemm("q_up", [KQL * 4 * B_QK] * 4, 8), Gemm("kv_up", [KKV * 4 * P] * 4, 8, dmas=[2 * KKV] * 4),
        Gemm("b_out", [KD * 256] * 4, 4), *mlp(1),
        *ffn(0), Gemm("pool", [8 * 256], 4, "act_evac"), *ffn(1),
        *ffn(2), Gemm("qkv", [KD * 256] * 12, 12), Gemm("w_o", [KD * 256] * 4, 4, "act_evac"), *ffn(3),
    ]
    chunk = unit = 0
    read = {"dve_evac": 0, "act_evac": 0}
    landed, total = [], [0, 0]
    for g in gemms:
        g.c0, g.u0, g.r0 = chunk, unit, read[g.reader]
        g.before = dict(read)
        chunk += len(g.sizes)
        unit += g.units
        read[g.reader] += g.units
        for k in g.dmas:
            total[len(landed) % 2] += 16 * k
            landed.append(total[len(landed) % 2])
    return {g.name: g for g in gemms}, [x for g in gemms for x in g.sizes], landed


def two_blocks_kernel(nc, A, consts, window, out):
    G, SIZES, LANDED = plan()
    N_CHUNKS = len(SIZES)
    ctx = ExitStack()
    with ctx:
        def sb(name, shape, dt=F32):
            return ctx.enter_context(nc.sbuf_tensor(name, shape, dt))

        def sem(name):
            return ctx.enter_context(nc.semaphore(name))

        cursor = [(nc.sbuf_base + 63) // 64 * 64]

        def place(name, shape, dt=F32, offset=None):
            size = 4 * int(np.prod(shape[1:]))
            if offset is None:
                offset = cursor[0]
                cursor[0] += (size + 31) // 32 * 32
                assert cursor[0] <= nc.sbuf_usable_end, name
            return nc.alloc_sbuf_tensor_at(name, shape, dt, offset=offset)

        raw = [place(f"w_raw{i}", [P, SLOT]) for i in range(2)]
        whi = [place(f"w_high{i}", [P, SLOT], F32R) for i in range(2)]
        wlo = [place(f"w_low{i}", [P, SLOT], F32R) for i in range(2)]
        X = place("x_state", [P, KD, T2])
        XH = place("xg_high", [P, KD, T2], F32R)
        XL = place("xg_low", [P, KD, T2], F32R)
        F = place("mixer_out", [P, KD, T2])
        cst = place("constants", [P, C_ALL])
        winv = place("window_inverse", [P, len(WINDOWS), T2])
        ones = place("ones", [P, P])
        gain = place("gains", [P, N_VEC_A + N_VEC_B])
        sq = [place(f"squares{i}", [P, 2, T2]) for i in range(2)]
        sqsum = place("square_sum", [P, T2])
        var = place("variance", [P, T2])
        guess = place("rstd_guess", [P, T2])
        step = place("rstd_step", [P, T2])
        rstd = place("rstd", [P, T2])
        ta = [place(f"evac_a{i}", [P, 2, T2]) for i in range(2)]
        tb = [place(f"evac_b{i}", [P, 2, T2]) for i in range(2)]
        cosA, sinA, cosB, sinB = (place(n, [P, SEQ]) for n in ("cos_a", "sin_a", "cos_b", "sin_b"))
        lam = place("lambda_cols", [P, 8])
        rowsum = place("row_sums", [P, 4, 2])
        rowneg = place("row_neg_max", [P, 4, 2])
        rowinv = place("row_inverse", [P, 4, 2])

        region = cursor[0]
        HH = place("hidden_high", [P, KF * SEQ], F32R)
        HL = place("hidden_low", [P, KF * SEQ], F32R)
        region_end = cursor[0]
        sub = [region]

        def alias(name, shape, dt=F32):
            t = place(name, shape, dt, offset=sub[0])
            sub[0] += 4 * int(np.prod(shape[1:]))
            assert sub[0] <= region_end, name
            return t

        Sm = [alias(f"scores{i}", [P, 2, T2]) for i in range(2)]
        Pr = [alias(f"probs{i}", [P, 2, T2]) for i in range(2)]
        PT = [alias(f"probs_T{i}", [P, 4, P]) for i in range(2)]
        O = alias("attn_out", [P, 2, D])
        per_layer = sub[0]
        qA = alias("a_q", [P, 8, SEQ])
        kA = alias("a_k", [P, 2, SEQ])
        vA = alias("a_v", [P, 2, KV_COLS])
        qiA = alias("a_qi", [P, 4, SEQ])
        kiA = alias("a_ki", [P, SEQ])
        wiF = alias("a_wi_features", [P, SEQ])
        wiA = alias("a_wi", [P, 2, IDX_HEADS])
        score = alias("a_score", [P, 2, SEQ])
        hide = alias("a_hide", [P, 2, SEQ])
        top8 = alias("a_top8", [P, 8])
        sub[0] = per_layer
        qB = alias("b_q", [P, B_HEADS, SEQ])
        kB = alias("b_k", [P, B_HEADS, SEQ])
        vB = alias("b_v", [P, 2, D])
        sub[0] = per_layer
        qC = alias("c_q", [P, DIFF_HEADS, SEQ])
        kC = alias("c_k", [P, DIFF_HEADS, T2])
        vC = alias("c_v", [P, 3, D])
        ssC = alias("c_square_sums", [P, 2, DIFF_HEADS])
        vaC = alias("c_variance", [P, 2, DIFF_HEADS])
        guC = alias("c_guess", [P, 2, DIFF_HEADS])
        stC = alias("c_step", [P, 2, DIFF_HEADS])
        rsC = alias("c_rstd", [P, 2, DIFF_HEADS])
        sub[0] = region
        PAD = max(WINDOWS)
        hnP = alias("pool_in", [P, KD, PAD + T2])
        win = [alias(f"pool_sum{i}", [P, KD, PAD + T2]) for i in range(2)]
        dfP = alias("pool_diff", [P, KD, T2])
        sub[0] = region
        meta_rows = alias("meta_rows", [META, D])
        vec_rows = [alias("vector_rows_a", [N_VEC_A, P]), alias("vector_rows_b", [N_VEC_B, P])]
        posi = alias("positions_int", [P, SEQ], I32)
        posf = alias("positions_float", [P, SEQ])
        ang = [alias(f"angle{i}", [P, SEQ]) for i in range(2)]
        turns = [alias(f"turns{i}", [P, SEQ]) for i in range(2)]
        half = [alias(f"half_sine{i}", [P, SEQ]) for i in range(2)]
        lrow = alias("lambda_rows", [P, 4, HD])
        lprod = alias("lambda_products", [P, 2, HD])

        xrows = F[:].rearrange("p k t -> p (k t)")[:, 0:2 * D].rearrange("p (i d) -> p i d", i=2)
        vF = F
        ident = cst[:, C_ID:C_ID + P]
        rotA, rotB = cst[:, C_RA:C_RA + P], cst[0:B_QK, C_RB:C_RB + B_QK]

        acc = [ctx.enter_context(nc.psum_tensor(f"acc{i}", [P, 2, 512], F32)) for i in range(2)]
        sp = [ctx.enter_context(nc.psum_tensor(f"spare{i}", [P, 2, 512], F32)) for i in range(2)]
        normps = sp[1][:, 1]

        rstd2 = place("rstd_second", [P, T2])
        names = """x_in meta_in vec_in const_in window_in pos_in lambda_in
            w_landed0 w_landed1 w_high w_low w_used dve_evac act_evac part_full
            ones_set xrow_turned vec_turned x_ready xg_high xg_ready sq_made sq_read norm_sum var_made
            guess_made dve_step act_step hid_high hid_ready gate_silu rope_turned kr_ready kr_spread
            angle_ready half_ready lam_ready lam_exp v_turned v_ready wi_in wi_turned wi_ready idx_full idx_relu idx_read
            s_full s_read exp_done probs_ready pt_full pt_ready o_full o_read o_all o_turned oT_high oT_ready
            q_ready k_ready c_var c_guess fg_ready pool_ready post_ready y_ready y_turned y_rows out_done""".split()
        S = {n: sem(n) for n in names}
        block = ctx.enter_context(nc.Block())

        @block.sync
        def _(sp_):
            def load_chunk(c, src, it=None, per=0, parts=None):
                if c >= 2 or it is not None:
                    sp_.wait_ge(S["w_low"], at(c - 1, it, per))
                dst = raw[c % 2]
                if parts is None:
                    k, n = src.shape[1], src.shape[2]
                    sp_.dma_start(dst[:, 0:k * n].rearrange("p (k n) -> p k n", k=k), src)\
                        .then_inc(S[f"w_landed{c % 2}"], 16)
                else:
                    k = src.shape[1]
                    wide = sum(n for _, n in parts)
                    v = dst[:, 0:k * wide].rearrange("p (k n) -> p k n", k=k)
                    o = 0
                    for j, (col, n) in enumerate(parts):
                        sp_.dma_start(v[:, :, o:o + n], src[:, :, col:col + n])\
                            .then_inc(S[f"w_landed{c % 2}"], 16)
                        o += n

            def rows(w):
                return w.rearrange("(k p) n -> p k n", p=P)

            def straight(name, w, n):
                for j in range(len(G[name].sizes)):
                    load_chunk(G[name].c0 + j, rows(w)[:, :, j * n:(j + 1) * n])

            def mlp(layer):
                up, down = G[f"mlp_up{layer}"], G[f"mlp_down{layer}"]
                w = rows(A["mlp_w_up"][layer])
                with sp_.Fori(0, KF // 4) as i:
                    for j in range(2):
                        load_chunk(up.c0 + j, w[:, :, ds(i * 512 + j * 256, 256)], i, 2)
                w = rows(A["mlp_w_down"][layer])
                with sp_.Fori(0, KD // 2) as i:
                    for j in range(4):
                        k0 = 16 * (j % 2)
                        load_chunk(down.c0 + j, w[:, k0:k0 + 16, ds(i * 2 * P + (j // 2) * P, P)], i, 4)

            def ffn(n):
                up, down = G[f"ffn_up{n}"], G[f"ffn_down{n}"]
                w = [rows(A[name][n // 2, n % 2]) for name in ("ffn_w1_2", "ffn_w3_2")]
                with sp_.Fori(0, KF2 // 2) as i:
                    for j in range(2):
                        load_chunk(up.c0 + j, w[j][:, :, ds(i * 256, 256)], i, 2)
                w = rows(A["ffn_w2_2"][n // 2, n % 2])
                with sp_.Fori(0, KD // 2) as i:
                    for j in range(2):
                        load_chunk(down.c0 + j, w[:, :, ds(i * 2 * P + j * P, P)], i, 2)

            for i in range(2):
                sp_.dma_start(xrows[:, i], A["x"][0, i * P:(i + 1) * P, :]).then_inc(S["x_in"], 16)
            w = rows(A["a_w_in"][0])
            c, qi0 = G["a_in"].c0, Q_COLS + 2 * KV_COLS
            ki0 = qi0 + QI_COLS
            for j in range(2):
                load_chunk(c + j, w[:, :, qi0 + 256 * j:qi0 + 256 * (j + 1)])
            load_chunk(c + 2, w, parts=[(ki0, HD), (ki0, HD), (ki0 + HD, IDX_HEADS)])
            for j in range(4):
                h = 8 * (j // 2) + 2 * (j % 2)
                load_chunk(c + 3 + j, w, parts=[(x * HD, HD) for x in (h, h + 4, h + 1, h + 5)])
            load_chunk(c + 7, w[:, :, Q_COLS:Q_COLS + KV_COLS])
            load_chunk(c + 8, w[:, :, Q_COLS + KV_COLS:Q_COLS + 2 * KV_COLS])
            straight("a_out", A["a_w_out"][0], 256)
            mlp(0)
            w = rows(A["b_w_in"][0])
            for j, (a, b) in enumerate(((0, 256), (256, 512), (512, 672))):
                load_chunk(G["b_in"].c0 + j, w[:, :, a:b])
            straight("q_up", A["b_w_q_up"][0], 4 * B_QK)
            for j in range(4):
                c = G["kv_up"].c0 + j
                sp_.wait_ge(S["w_low"], c - 1)
                src = rows(A["b_w_kv_up"][0])[:, :, j * 4 * P:(j + 1) * 4 * P]
                for k in range(KKV):
                    for t in range(2):
                        dst = raw[c % 2][:, (2 * k + t) * 2 * P:(2 * k + t + 1) * 2 * P]
                        sp_.dma_start(dst.rearrange("p (h d) -> p h d", h=4),
                                      src[:, k].rearrange("p (h t d) -> p h t d", h=4, t=2)[:, :, t])\
                            .then_inc(S[f"w_landed{c % 2}"], 16)
            straight("b_out", A["b_w_out"][0], 256)
            mlp(1)
            ffn(0)
            load_chunk(G["pool"].c0, A["pool_w_2"][0].rearrange("g (k p) n -> p (g k) n", p=P))
            ffn(1)
            ffn(2)
            straight("qkv", A["attn_w_qkv_2"][0], 256)
            straight("w_o", A["attn_w_o_2"][0], 256)
            ffn(3)
            for i in range(2):
                sp_.wait_ge(S["y_rows"], 2 * (i + 1))
                sp_.dma_start(out[0, i * P:(i + 1) * P, :], xrows[:, i]).then_inc(S["out_done"], 16)
            sp_.wait_ge(S["out_done"], 32)

        @block.gpsimd
        def _(pool):
            pool.memset(ones[:], 1.0).then_inc(S["ones_set"], 1)
            pool.wait_ge(S["kr_ready"], 1)
            for h in range(1, B_HEADS):
                ins = pool.tensor_copy(kB[B_NOPE:B_QK, h, :], kB[B_NOPE:B_QK, 0, :])
            ins.then_inc(S["kr_spread"], 1)

        @block.tensor
        def _(pe):
            n = Counts()

            def begin(g):
                for name, value in g.before.items():
                    if value:
                        pe.wait_ge(S[name], value)

            def wait_unit(g, j, it=None, per=0):
                if j >= 2:
                    pe.wait_ge(S[g.reader], at(g.r0 + j - 1, it, per))

            def three(dst, high_w, low_w, high, low, first, last):
                pe.matmul(dst, high_w, high, start=first, stop=False)
                pe.matmul(dst, high_w, low, start=False, stop=False)
                return pe.matmul(dst, low_w, high, start=False, stop=last)

            def cols(c, a, b):
                return whi[c % 2][:, a:b], wlo[c % 2][:, a:b]

            def sum_squares(T, groups):
                pe.wait_ge(S["sq_read"], n.add("sq_read", groups))
                pe.matmul(normps[:, 0:T], ones[:], sqsum[:, 0:T], start=True, stop=True)\
                    .then_inc(S["norm_sum"], 1)

            def wide(g, j, T0, T, ready=None, it=None, per=0, tiles=None):
                c, u = g.c0 + j, g.u0 + j
                pe.wait_ge(S["w_low"], at(c + 1, it, per))
                wait_unit(g, j, it, per)
                for k in range(KD):
                    if ready is not None and ready[k] is not None:
                        pe.wait_ge(*ready[k])
                    for m in range(2):
                        if tiles is None:
                            w, rows_ = cols(c, k * 256 + m * P, k * 256 + (m + 1) * P), P
                        else:
                            w, rows_ = tiles(c, k, m)
                        ins = three(acc[u % 2][0:rows_, m, 0:T], *w, XH[:, k, T0:T0 + T], XL[:, k, T0:T0 + T],
                                    k == 0, k == KD - 1)
                ins.then_inc(S["w_used"], 1)

            def xg_waits(groups):
                waits = [None] * KD
                for a, b in groups:
                    waits[a] = (S["xg_ready"], n.add("xg_ready"))
                return waits

            def oT_waits():
                waits = [None] * KD
                waits[0] = (S["oT_ready"], n.add("oT_ready", 4))
                return waits

            def turn_rope(g, j, rows_, tiles, rot):
                u = g.u0 + j
                pe.wait_ge(S["dve_evac"], g.r0 + j + 1)
                pe.matmul(sp[0][0:rows_, u % 2, 0:tiles * SEQ], rot, ta[u % 2][0:rows_, 0:tiles, 0:SEQ],
                          start=True, stop=True).then_inc(S["rope_turned"], 1)

            def down(g, T, K, chunks):
                kc = K // chunks

                def unit(j, it=None):
                    u = g.u0 + j
                    wait_unit(g, j, it, 2)
                    for q in range(chunks):
                        c = g.c0 + j * chunks + q
                        pe.wait_ge(S["w_low"], at(c + 1, it, 2 * chunks))
                        for k in range(kc):
                            h = (q * kc + k) * T
                            ins = three(acc[u % 2][:, 0, 0:T], *cols(c, k * P, (k + 1) * P), HH[:, h:h + T],
                                        HL[:, h:h + T], q == 0 and k == 0, q == chunks - 1 and k == kc - 1)
                        ins.then_inc(S["w_used"], 1)

                begin(g)
                pe.wait_ge(S["hid_ready"], n.get("hid_ready"))
                for j in range(2):
                    unit(j)
                with pe.Fori(0, KD // 2 - 1) as i:
                    for j in range(2, 4):
                        unit(j, i)

            SINGLES = [(k, k + 1) for k in range(KD)]
            PAIRS = [(k, k + 2) for k in range(0, KD, 2)]

            def up(g, T0, T, groups, outputs, squares=4):
                begin(g)
                wide(g, 0, T0, T, xg_waits(groups))
                sum_squares(T, squares)
                wide(g, 1, T0, T)
                with pe.Fori(0, g.units // 2 - 1) as i:
                    for j in range(2, 4):
                        wide(g, j, T0, T, it=i, per=2)
                n.add("hid_ready", outputs)

            def mlp(layer):
                up(G[f"mlp_up{layer}"], META, SEQ, PAIRS, KF // 2)
                down(G[f"mlp_down{layer}"], SEQ, KF, 2)

            def ffn(i, T0, T):
                up(G[f"ffn_up{i}"], T0, T, PAIRS, KF2 // 2)
                down(G[f"ffn_down{i}"], T, KF2, 1)
                sum_squares(T, KD)

            def turn_v(g, tiles, token_tiles, src=vF):
                pe.wait_ge(S["dve_evac"], g.r0 + g.units)
                done = n.get("v_ready")
                q = 0
                for t0, nt in token_tiles:
                    for first in range(0, tiles, 4):
                        if q >= 4:
                            pe.wait_ge(S["v_ready"], done + q - 3)
                        for m in range(first, min(first + 4, tiles)):
                            ins = pe.transpose(sp[(q // 2) % 2][0:nt, q % 2, (m - first) * P:(m - first + 1) * P],
                                               src[:, m, t0:t0 + nt], ident)
                        ins.then_inc(S["v_turned"], 1)
                        q += 1
                pe.wait_ge(S["v_ready"], n.add("v_ready", q))

            def attention(pieces, scores, prob_tiles, values, probs_by):
                s0, t0, r0, o0 = n.get("s_read"), n.get("pt_ready"), n.get("probs"), n.get("o_read")

                def make_scores(p):
                    if p >= 2:
                        pe.wait_ge(S["s_read"], s0 + p - 1)
                    for c, (q, k) in enumerate(scores(*pieces[p])):
                        ins = pe.matmul(sp[p % 2][:, c, 0:k.shape[1]], q, k, start=True, stop=True)
                    ins.then_inc(S["s_full"], 1)

                def turn_probs(p):
                    pe.wait_ge(S[probs_by], n.add(probs_by))
                    if p >= 2:
                        pe.wait_ge(S["pt_ready"], t0 + p - 1)
                    for slot, (c, k0, nk) in enumerate(prob_tiles(pieces[p][0])):
                        ins = pe.transpose(acc[0][0:nk, p % 2, slot * P:(slot + 1) * P], Pr[p % 2][:, c, k0:k0 + nk],
                                           ident)
                    ins.then_inc(S["pt_full"], 1)

                def make_out(p):
                    pe.wait_ge(S["pt_ready"], t0 + p + 1)
                    if p >= 2:
                        pe.wait_ge(S["o_read"], o0 + p - 1)
                    tiles = prob_tiles(pieces[p][0])
                    for slot, (c, k0, nk) in enumerate(tiles):
                        v = values(*pieces[p], c, k0 // P, nk)
                        w = v.shape[1]
                        first = slot == 0 or tiles[slot - 1][0] != c
                        last = slot == len(tiles) - 1 or tiles[slot + 1][0] != c
                        ins = pe.matmul(acc[1][:, p % 2, c * w:(c + 1) * w], PT[p % 2][0:nk, slot, :], v,
                                        start=first, stop=last)
                    ins.then_inc(S["o_full"], 1)

                N = len(pieces)
                make_scores(0)
                for p in range(N):
                    if p + 1 < N:
                        make_scores(p + 1)
                    turn_probs(p)
                    if p >= 1:
                        make_out(p - 1)
                make_out(N - 1)
                n.add("s_read", N)
                n.add("pt_ready", N)
                n.add("o_read", N)

            def turn_out(signal, value):
                pe.wait_ge(S[signal], value)
                for i in range(2):
                    for half in range(2):
                        for k in range(4):
                            ins = pe.transpose(sp[i][:, half, k * P:(k + 1) * P],
                                               O[:, i, (4 * half + k) * P:(4 * half + k + 1) * P], ident)
                        ins.then_inc(S["o_turned"], 1)

            pe.wait_ge(S["const_in"], 16)
            pe.wait_ge(S["x_in"], 32)
            for i in range(2):
                for halfk in range(2):
                    for k in range(4):
                        ins = pe.transpose(acc[i][:, halfk, k * P:(k + 1) * P],
                                           xrows[:, i, (4 * halfk + k) * P:(4 * halfk + k + 1) * P], ident)
                    ins.then_inc(S["xrow_turned"], 1)
            pe.wait_ge(S["vec_in"], 16 * (len(VEC_A) + len(VEC_B)))
            pe.wait_ge(S["meta_in"], 16)
            for j, rows_ in enumerate((N_VEC_A, N_VEC_B)):
                pe.transpose(sp[1][:, j, 0:rows_], vec_rows[j][:, :], ident[0:rows_, 0:rows_])
            for k in range(KD):
                ins = pe.transpose(sp[0][:, 0, k * META:(k + 1) * META], meta_rows[:, k * P:(k + 1) * P],
                                   ident[0:META, 0:META])
            ins.then_inc(S["vec_turned"], 1)

            g = G["a_in"]
            pe.wait_ge(S["ones_set"], 1)
            wide(g, 0, META, SEQ, xg_waits(PAIRS))
            sum_squares(SEQ, 4)
            wide(g, 1, META, SEQ)
            turn_rope(g, 0, P, 2, rotA)

            def key_and_weights(c, k, m):
                a = k * 136 + m * P
                return cols(c, a, a + (P if m == 0 else IDX_HEADS)), (P if m == 0 else IDX_HEADS)

            wide(g, 2, META, SEQ, tiles=key_and_weights)
            turn_rope(g, 1, P, 2, rotA)
            for j in range(3, 7):
                wide(g, j, META, SEQ)
                turn_rope(g, j - 1, P, 1 if j == 3 else 2, rotA)
            wide(g, 7, META, SEQ)
            turn_rope(g, 6, P, 2, rotA)
            wide(g, 8, META, SEQ)
            turn_rope(g, 7, P, 2, rotA)

            pe.wait_ge(S["wi_in"], 1)
            for i in range(2):
                ins = pe.transpose(sp[1][:, 0, i * IDX_HEADS:(i + 1) * IDX_HEADS],
                                   wiF[0:IDX_HEADS, i * P:(i + 1) * P], ident[0:IDX_HEADS, 0:IDX_HEADS])
            ins.then_inc(S["wi_turned"], 1)
            pe.wait_ge(S["q_ready"], n.add("q_ready"))
            turn_v(g, 2, [(0, P), (P, P)])
            for q in range(8):
                i, m = q // 4, q % 4
                if q == 1:
                    pe.wait_ge(S["wi_ready"], 1)
                if q >= 2:
                    pe.wait_ge(S["idx_relu"], q - 1)
                for c in range(2):
                    r = slice(c * HD, (c + 1) * HD)
                    ins = pe.matmul(sp[q % 2][:, c, 0:(i + 1) * P], qiA[r, m, i * P:(i + 1) * P],
                                    kiA[r, 0:(i + 1) * P], start=True, stop=True)
                ins.then_inc(S["idx_full"], 1)
            pe.wait_ge(S["idx_relu"], 8)

            def halves(i):
                return [(c, k * P, P) for c in range(2) for k in range(i + 1)]

            begin(G["a_out"])
            attention([(i, m) for m in range(8) for i in range(2)],
                      lambda i, m: [(qA[c * HD:(c + 1) * HD, m, i * P:(i + 1) * P],
                                     kA[c * HD:(c + 1) * HD, m // 4, 0:(i + 1) * P]) for c in range(2)],
                      halves,
                      lambda i, m, c, kt, nk: vA[:, kt, (2 * (m // 4) + c) * HD:(2 * (m // 4) + c + 1) * HD],
                      "exp_done")
            turn_out("o_read", n.get("o_read"))
            g = G["a_out"]
            for j in range(4):
                wide(g, j, META, SEQ, oT_waits() if j == 0 else None)
            mlp(0)

            g = G["b_in"]
            begin(g)
            wide(g, 0, META, SEQ, xg_waits(SINGLES))
            sum_squares(SEQ, KD)
            wide(g, 1, META, SEQ)

            def latent_and_key(c, k, m):
                a = k * 160 + m * B_NOPE
                return cols(c, a, a + (P if m == 0 else B_QK)), (P if m == 0 else B_QK)

            wide(g, 2, META, SEQ, tiles=latent_and_key)
            turn_rope(g, 2, B_QK, 1, rotB)

            def latent_unit(g, j, last, tiles, k0, KK, rows_, it=None):
                u = g.u0 + j
                wait_unit(g, j)
                for t, (dst, weights) in enumerate(tiles(u)):
                    for k in range(KK):
                        ins = three(dst, *weights(k), XH[:, k0 + k, META:META + SEQ], XL[:, k0 + k, META:META + SEQ],
                                    k == 0, k == KK - 1)
                ins.then_inc(S["w_used" if last else "part_full"], 1)

            g = G["q_up"]
            begin(g)
            for group in ((0, 2), (2, 3)):
                n.add("xg_ready")
            pe.wait_ge(S["xg_ready"], n.get("xg_ready"))
            sum_squares(SEQ, 2)
            for j in range(8):
                c = g.c0 + j // 2
                if j % 2 == 0:
                    pe.wait_ge(S["w_low"], c + 1)

                def heads(u, c=c, r=j % 2):
                    for m in range(2):
                        def weights(k, m=m):
                            a = k * 4 * B_QK + (2 * r + m) * B_QK
                            return cols(c, a, a + B_QK)
                        yield acc[u % 2][0:B_QK, m, 0:SEQ], weights
                latent_unit(g, j, j % 2 == 1, heads, 0, KQL, B_QK)
                if j == 0:
                    sum_squares(SEQ, 1)
                if j >= 1:
                    turn_rope(g, j - 1, B_QK, 2, rotB)
            turn_rope(g, 7, B_QK, 2, rotB)
            g = G["kv_up"]
            begin(g)
            pe.wait_ge(S["xg_ready"], n.add("xg_ready"))
            for j in range(8):
                c = g.c0 + j // 2
                if j % 2 == 0:
                    pe.wait_ge(S["w_low"], c + 1)

                def keys(u, c=c):
                    for h in range(4):
                        yield (acc[u % 2][0:B_NOPE, h // 2, (h % 2) * SEQ:(h % 2 + 1) * SEQ],
                               lambda k, h=h: cols(c, k * 4 * P + h * B_NOPE, k * 4 * P + (h + 1) * B_NOPE))

                def vals(u, c=c):
                    for m in range(2):
                        yield (acc[u % 2][:, m, 0:SEQ],
                               lambda k, m=m: cols(c, k * 4 * P + (m + 2) * P, k * 4 * P + (m + 3) * P))
                latent_unit(g, j, j % 2 == 1, keys if j % 2 == 0 else vals, KQL, KKV, P)
            pe.wait_ge(S["q_ready"], n.add("q_ready"))
            turn_v(g, 8, [(0, P), (P, P)])
            pe.wait_ge(S["kr_spread"], 1)
            begin(G["b_out"])
            attention([(i, m) for m in range(8) for i in range(2)],
                      lambda i, m: [(qB[0:B_QK, 2 * m + c, i * P:(i + 1) * P],
                                     kB[0:B_QK, 2 * m + c, 0:(i + 1) * P]) for c in range(2)],
                      halves,
                      lambda i, m, c, kt, nk: vB[:, kt, (2 * m + c) * B_V:(2 * m + c + 1) * B_V],
                      "exp_done")
            turn_out("o_read", n.get("o_read"))
            g = G["b_out"]
            for j in range(4):
                wide(g, j, META, SEQ, oT_waits() if j == 0 else None)
            mlp(1)
            sum_squares(SEQ, KD)

            ffn(0, 0, T2)
            sum_squares(T2, 4)
            g = G["pool"]
            begin(g)
            pe.wait_ge(S["w_low"], g.c0 + 1)
            pe.wait_ge(S["xg_ready"], n.add("xg_ready"))
            for j in range(4):
                u = g.u0 + j
                wait_unit(g, j)
                for m in range(2):
                    for k in range(2):
                        a = (2 * j + k) * 256 + m * P
                        ins = three(acc[u % 2][:, m, 0:T2], *cols(g.c0, a, a + P), XH[:, 2 * j + k, :],
                                    XL[:, 2 * j + k, :], k == 0, k == 1)
                ins.then_inc(S["w_used" if j == 3 else "part_full"], 1)
            sum_squares(T2, 4)
            ffn(1, 0, T2)
            ffn(2, 0, T2)
            g = G["qkv"]
            begin(g)
            wide(g, 0, 0, T2, xg_waits(PAIRS))
            sum_squares(T2, 4)
            for j in range(1, 12):
                wide(g, j, 0, T2)
            turn_v(g, 8, [(0, P), (P, P), (2 * P, META)])
            begin(G["w_o"])
            attention([(i, h) for h in range(DIFF_HEADS) for i in range(2)],
                      lambda i, h: [(qC[c * HD:(c + 1) * HD, h, i * P:(i + 1) * P],
                                     kC[c * HD:(c + 1) * HD, h, 0:(i + 1) * P + META]) for c in range(2)],
                      lambda i: [(0, k * P, P) for k in range(i + 1)] + [(0, (i + 1) * P, META)],
                      lambda i, h, c, kt, nk: vC[0:nk, kt, h * P:(h + 1) * P],
                      "probs_ready")
            turn_out("o_all", 1)
            g = G["w_o"]
            for j in range(4):
                wide(g, j, META, SEQ, oT_waits() if j == 0 else None)
            sum_squares(SEQ, 4)
            ffn(3, META, SEQ)
            pe.wait_ge(S["y_ready"], 4)
            for i in range(2):
                for halfk in range(2):
                    for k in range(4):
                        ins = pe.transpose(acc[i][:, halfk, k * P:(k + 1) * P],
                                           X[:, 4 * halfk + k, META + i * P:META + (i + 1) * P], ident)
                    ins.then_inc(S["y_turned"], 1)

        SINGLES = [(k, k + 1) for k in range(KD)]
        PAIRS = [(k, k + 2) for k in range(0, KD, 2)]
        
        def unit_full(g, j):
            if g.name in ("q_up", "kv_up", "pool"):
                per_chunk = g.units // len(g.sizes)
                if j % per_chunk < per_chunk - 1:
                    done = {"q_up": 0, "kv_up": 4, "pool": 8}[g.name]
                    return S["part_full"], done + j // per_chunk * (per_chunk - 1) + j % per_chunk + 1
                return S["w_used"], g.c0 + j // per_chunk + 1
            chunks = len(g.sizes) // g.units
            return S["w_used"], g.c0 + (j + 1) * chunks

        @block.scalar
        def _(act):
            n = Counts()

            def link(ins):
                ins.then_inc(S["act_step"], 1)
                act.wait_ge(S["act_step"], n.add("act_step"))

            def split(c, it=None, per=0):
                if c >= N_CHUNKS:
                    return
                act.wait_ge(S[f"w_landed{c % 2}"], at(LANDED[c], it, 8 * per))
                if c >= 2:
                    act.wait_ge(S["w_used"], at(c - 1, it, per))
                act.activation(whi[c % 2][:, 0:SIZES[c]], raw[c % 2][:, 0:SIZES[c]], ACT.Copy).then_inc(S["w_high"], 1)

            def xg(groups, gcol, T0, T, width, src=None, waits=None, high=True, after=None):
                src = src or X
                for q, (a, b) in enumerate(groups):
                    if after is not None:
                        act.wait_ge(S["dve_evac"], after.r0 + q + 1)
                    elif waits[q]:
                        act.wait_ge(S["x_ready"], n.add("x_ready", waits[q]))
                    if high:
                        for k in range(a, b):
                            ins = act.activation(XH[:, k, T0:T0 + T], src[:, k, T0:T0 + T], ACT.Identity,
                                                 scale=gain[:, gcol + k - groups[0][0]:gcol + k - groups[0][0] + 1])
                        ins.then_inc(S["xg_high"], 1)
                    par = n.add("squares") % 2
                    if n.get("squares") > 2:
                        act.wait_ge(S["sq_read"], n.get("squares") - 2)
                    act.activation(sq[par][:, 0:b - a, 0:T], src[:, a:b, T0:T0 + T], ACT.Square,
                                   scale=width ** -0.5).then_inc(S["sq_made"], 1)

            def root(T):
                act.wait_ge(S["var_made"], n.add("var_made"))
                link(act.activation(guess[:, 0:T], var[:, 0:T], ACT.Ln))
                act.activation(guess[:, 0:T], guess[:, 0:T], ACT.Exp, scale=-0.5).then_inc(S["guess_made"], 1)

            def mlp(layer, gcol):
                g = G[f"mlp_up{layer}"]

                def unit(j, it=None):
                    if j or it is not None:
                        split(g.c0 + j + 2, it, 2)
                    par = j % 2
                    act.wait_ge(S["dve_evac"], at(g.r0 + j + 1, it, 2))
                    act.activation(tb[par][:, :, 0:SEQ], ta[par][:, :, 0:SEQ], ACT.Square).then_inc(S["act_step"], 1)
                    act.wait_ge(S["act_step"], at(step0 + j + 1, it, 2))
                    h = 2 * j * SEQ
                    dst = HH[:, h:h + 2 * SEQ] if it is None else HH[:, ds(it * 4 * SEQ + h, 2 * SEQ)]
                    act.activation(dst.rearrange("p (k t) -> p k t", k=2), tb[par][:, :, 0:SEQ], ACT.Copy)\
                        .then_inc(S["hid_high"], 1)

                split(g.c0 + 2)
                root(SEQ)
                step0 = n.get("act_step")
                unit(0)
                unit(1)
                with act.Fori(0, g.units // 2 - 2) as i:
                    for j in range(2, 4):
                        unit(j, i)
                for j in range(g.units - 2, g.units):
                    unit(j)
                n.add("act_step", g.units)
                g = G[f"mlp_down{layer}"]
                sq0 = n.get("squares")

                def unit(j, it=None):
                    for q in range(2):
                        split(g.c0 + 2 * j + q + 2, it, 4)
                    act.wait_ge(S["sq_read"], at(sq0 + j - 1, it, 2))
                    act.wait_ge(S["dve_evac"], at(g.r0 + j + 1, it, 2))
                    if gcol is not None:
                        dst = XH[:, j, META:] if it is None else XH[:, ds(it * 2 + j, 1), META:]
                        src = X[:, j, META:] if it is None else X[:, ds(it * 2 + j, 1), META:]
                        sc = gain[:, gcol + j:gcol + j + 1] if it is None else gain[:, ds(it * 2 + gcol + j, 1)]
                        act.activation(dst, src, ACT.Identity, scale=sc).then_inc(S["xg_high"], 1)
                    par = (sq0 + j + 1) % 2
                    src = X[:, j:j + 1, META:] if it is None else X[:, ds(it * 2 + j, 1), META:]
                    act.activation(sq[par][:, 0:1, 0:SEQ], src, ACT.Square, scale=D ** -0.5).then_inc(S["sq_made"], 1)

                with act.Fori(0, KD // 2 - 1) as i:
                    for j in range(2):
                        unit(j, i)
                for j in range(KD - 2, KD):
                    unit(j)
                n.add("squares", KD)

            def post_unit(g, j, dst, bank, gcols, T, sq0, it=None, per=0):
                sem_, value = unit_full(g, j)
                act.wait_ge(sem_, at(value, it, per))
                for m, (d, gc) in enumerate(zip(dst, gcols)):
                    act.activation(d, bank[:, m, 0:T], ACT.Identity, scale=gc)
                par = (sq0 + j + 1) % 2
                if sq0 + j + 1 > 2:
                    act.wait_ge(S["sq_read"], at(sq0 + j - 1, it, per))
                act.activation(sq[par][:, 0:len(dst), 0:T], bank[:, 0:len(dst), 0:T], ACT.Square,
                               scale=D ** -0.5).then_inc(S["act_evac"], 1)

            def ffn(i, T0, T, post):
                g = G[f"ffn_up{i}"]
                h0 = n.get("up_value")

                def pair(j, it=None, first=False):
                    split(g.c0 + j + 2, it, 2)
                    if first:
                        root(T)
                        act.preload_act_table_set("silu_and_others")
                    act.wait_ge(S["dve_evac"], at(g.r0 + j + 1, it, 2))
                    act.activation(tb[0][:, :, 0:T], ta[0][:, :, 0:T], ACT.Silu).then_inc(S["gate_silu"], 1)
                    split(g.c0 + j + 3, it, 2)
                    act.wait_ge(S["dve_evac"], at(g.r0 + j + 2, it, 2))
                    h = j * T
                    dst = HH[:, h:h + 2 * T] if it is None else HH[:, ds(it * 2 * T + h, 2 * T)]
                    act.activation(dst.rearrange("p (k t) -> p k t", k=2), tb[1][:, :, 0:T], ACT.Copy)\
                        .then_inc(S["hid_high"], 1)

                pair(0, first=True)
                with act.Fori(0, g.units // 2 - 2) as it:
                    pair(2, it)
                pair(g.units - 2)
                act.preload_act_table_set("natural_log_exp_and_others")
                g = G[f"ffn_down{i}"]
                sq0 = n.get("squares")

                def unit(j, it=None):
                    split(g.c0 + j + 2, it, 2)
                    gcol = GAIN["ffn_norm_post_2"] + i * KD + j
                    dst = F[:, j, T0:T0 + T] if it is None else F[:, ds(it * 2 + j, 1), T0:T0 + T]
                    gc = gain[:, gcol:gcol + 1] if it is None else gain[:, ds(it * 2 + gcol, 1)]
                    post_unit(g, j, [dst], acc[(g.u0 + j) % 2], [gc], T, sq0, it, 2)

                with act.Fori(0, KD // 2 - 1) as it:
                    for j in range(2):
                        unit(j, it)
                for j in range(KD - 2, KD):
                    unit(j)
                n.add("squares", KD)
                root(T)

            def copy_v(dst):
                for q, (pieces, d) in enumerate(dst):
                    act.wait_ge(S["v_turned"], n.add("v_turned"))
                    act.activation(d, pieces, ACT.Copy).then_inc(S["v_ready"], 1)

            def attention(pieces, keys, slots, outs):
                s0, t0, a0, o0 = n.get("s_read"), n.get("pt_full"), n.get("probs_taken"), n.get("o_full")

                def exps(p):
                    act.wait_ge(S["s_read"], s0 + p + 1)
                    if p >= 2:
                        act.wait_ge(S["pt_full"], t0 + p - 1)
                    nk = keys(pieces[p][0])
                    for c in range(2):
                        ins = act.activation(Pr[p % 2][:, c, 0:nk], Sm[p % 2][:, c, 0:nk], ACT.Exp,
                                             bias=rowneg[:, p % 4, c:c + 1], accum_out=rowsum[:, p % 4, c:c + 1])
                    ins.then_inc(S["exp_done"], 1)

                def turned(p):
                    act.wait_ge(S["pt_full"], t0 + p + 1)
                    if p >= 2:
                        act.wait_ge(S["o_full"], o0 + p - 1)
                    for k0, k1, rows_ in slots(pieces[p][0]):
                        ins = act.activation(PT[p % 2][0:rows_, k0:k1, :], acc[0][0:rows_, p % 2, k0 * P:k1 * P]
                                             .rearrange("p (k t) -> p k t", t=P), ACT.Copy)
                    ins.then_inc(S["pt_ready"], 1)

                N = len(pieces)
                for p in range(N):
                    exps(p)
                    if p >= 1:
                        turned(p - 1)
                    if outs and p >= 2:
                        outs(p - 2, *pieces[p - 2])
                turned(N - 1)
                if outs:
                    outs(N - 2, *pieces[N - 2])
                    outs(N - 1, *pieces[N - 1])
                n.add("s_read", N)
                n.add("pt_full", N)
                n.add("o_full", N)

            def out_high(gcol=None):
                for i in range(2):
                    for half_ in range(2):
                        act.wait_ge(S["o_turned"], n.add("o_turned"))
                        dst = XH[:, 4 * half_:4 * half_ + 4, META + i * P:META + (i + 1) * P]
                        src = sp[i][:, half_, :].rearrange("p (k t) -> p k t", k=4)
                        if gcol is None:
                            ins = act.activation(dst, src, ACT.Copy)
                        else:
                            ins = act.activation(dst, src, ACT.Identity, scale=gain[:, gcol:gcol + 1])
                        ins.then_inc(S["oT_high"], 1)

            act.dma_start(cst[:], consts).then_inc(S["const_in"], 16)
            for rows_, table in zip(vec_rows, (VEC_A, VEC_B)):
                a = 0
                for name, k in table:
                    src = A[name]
                    dims = len(src.shape)
                    flat = src if dims == 1 else src.rearrange(" ".join("abcd"[:dims]) + " -> (" +
                                                               " ".join("abcd"[:dims]) + ")")
                    act.dma_start(rows_[a:a + k, :], flat.rearrange("(k p) -> k p", p=P)).then_inc(S["vec_in"], 16)
                    a += k
            act.dma_start(meta_rows[:], A["meta_tokens_2"]).then_inc(S["meta_in"], 16)
            act.dma_start(posi[:], A["positions"].rearrange("a t -> (a t)").partition_broadcast(P))\
                .then_inc(S["pos_in"], 16)
            for j, name in enumerate(("q1", "k1", "q2", "k2")):
                act.dma_start(lrow[:, j], A[f"attn_lambda_{name}_2"].rearrange("a d -> (a d)").partition_broadcast(P))\
                    .then_inc(S["lambda_in"], 16)
            act.dma_start(winv[:].rearrange("p w t -> p (w t)"), window.rearrange("w t -> (w t)")
                          .partition_broadcast(P)).then_inc(S["window_in"], 16)

            for r, (sn, hf) in enumerate(((sinA, half[0]), (sinB, half[1]))):
                act.wait_ge(S["angle_ready"], r + 1)
                act.activation(sn[:], ang[r][:], ACT.Sin)
                act.activation(hf[:], ang[r][:], ACT.Sin, scale=0.5).then_inc(S["half_ready"], 1)
            act.preload_act_table_set("natural_log_exp_and_others")
            act.wait_ge(S["lam_ready"], 1)
            act.activation(lam[:, 2:4], lam[:, 0:2], ACT.Exp).then_inc(S["lam_exp"], 1)
            split(0)
            xg(PAIRS, GAIN["attn_norm"], META, SEQ, D, waits=[4, 0, 0, 0])
            split(1)

            g = G["a_in"]
            split(2)
            root(SEQ)
            for j in range(1, 9):
                split(g.c0 + j + 2)
            copy_v([(sp[0][:, i, 0:KV_COLS], vA[:, i, :]) for i in range(2)])
            for q in range(8):
                act.wait_ge(S["idx_full"], q + 1)
                if q >= 2:
                    act.wait_ge(S["idx_read"], q - 1)
                nk = (q // 4 + 1) * P
                act.activation(Sm[q % 2][:, :, 0:nk], sp[q % 2][:, :, 0:nk], ACT.Relu).then_inc(S["idx_relu"], 1)
            pieces = [(i, m) for m in range(8) for i in range(2)]
            attention(pieces, lambda i: (i + 1) * P, lambda i: [(0, 2 * (i + 1), P)], None)
            out_high()
            for j in range(4):
                split(G["a_out"].c0 + j + 2)
            xg(PAIRS, GAIN["mlp_norm"], META, SEQ, D, after=G["a_out"])
            mlp(0, GAIN["attn_norm"] + KD)

            g = G["b_in"]
            split(g.c0 + 2)
            root(SEQ)
            split(g.c0 + 3)
            split(g.c0 + 4)
            xg([(0, 2), (2, 3)], GAIN["b_q_norm"], META, SEQ, B_QL, src=Flat(F, META), waits=[1, 0])
            xg([(3, 5)], GAIN["b_kv_norm"], META, SEQ, B_KVL, src=Flat(F, META), waits=[0])
            root(SEQ)
            for j in range(4):
                split(G["q_up"].c0 + j + 2)
                if j == 0:
                    root(SEQ)
            for j in range(4):
                split(G["kv_up"].c0 + j + 2)
            copy_v([(sp[i][:, h, :], vB[:, i, h * 512:(h + 1) * 512]) for i in range(2) for h in range(2)])
            attention(pieces, lambda i: (i + 1) * P, lambda i: [(0, 2 * (i + 1), P)], None)
            out_high()
            for j in range(4):
                split(G["b_out"].c0 + j + 2)
            xg(PAIRS, GAIN["mlp_norm"] + KD, META, SEQ, D, after=G["b_out"])
            mlp(1, None)
            root(SEQ)

            PRE, POST = GAIN["ffn_norm_pre_2"], GAIN["ffn_norm_post_2"]
            xg(PAIRS, PRE, 0, T2, D, waits=[1] * 4)
            ffn(0, 0, T2, POST)
            xg(PAIRS, None, 0, T2, D, waits=[1] * 4, high=False)
            root(T2)
            act.wait_ge(S["pool_ready"], 1)
            act.activation(XH[:].rearrange("p k t -> p (k t)"), dfP[:].rearrange("p k t -> p (k t)"), ACT.Copy)\
                .then_inc(S["xg_high"], 1)
            g = G["pool"]
            sq0 = n.get("squares")
            for j in range(4):
                sem_, value = unit_full(g, j)
                act.wait_ge(sem_, value)
                bank = acc[(g.u0 + j) % 2]
                for m in range(2):
                    k = 2 * j + m
                    ins = act.activation(ta[j % 2][:, m, :], bank[:, m, 0:T2], ACT.Identity,
                                         scale=gain[:, GAIN["pool_scale_2"] + k:GAIN["pool_scale_2"] + k + 1],
                                         bias=gain[:, GAIN["pool_b_2"] + k:GAIN["pool_b_2"] + k + 1])
                ins.then_inc(S["act_evac"], 1)
                act.wait_ge(S["act_evac"], g.r0 + j + 1)
                for m in range(2):
                    k = 2 * j + m
                    gc = GAIN["mix_norm_post_2"] + k
                    act.activation(F[:, k, :], ta[j % 2][:, m, :], ACT.Identity, scale=gain[:, gc:gc + 1])
                par = n.add("squares") % 2
                act.wait_ge(S["sq_read"], n.get("squares") - 2)
                act.activation(sq[par][:], ta[j % 2][:], ACT.Square, scale=D ** -0.5).then_inc(S["sq_made"], 1)
                if j == 3:
                    split(g.c0 + 2)
            root(T2)
            xg(PAIRS, PRE + KD, 0, T2, D, waits=[1] * 4)
            ffn(1, 0, T2, POST + KD)
            xg(PAIRS, PRE + 2 * KD, 0, T2, D, waits=[1] * 4)
            ffn(2, 0, T2, POST + 2 * KD)
            xg(PAIRS, GAIN["mix_norm_pre_2"] + KD, 0, T2, D, waits=[1] * 4)
            g = G["qkv"]
            split(g.c0 + 2)
            root(T2)
            for j in range(1, 12):
                split(g.c0 + j + 2)
            copy_v([(sp[i % 2][0:nt, h, :], vC[0:nt, i, h * 512:(h + 1) * 512])
                    for i, nt in enumerate((P, P, META)) for h in range(2)])
            pieces = [(i, h) for h in range(DIFF_HEADS) for i in range(2)]

            def squares_of_out(p, i, h):
                act.wait_ge(S["o_full"], n.get("o_full") + p + 1)
                if p:
                    act.wait_ge(S["o_read"], 2 * len(pieces) + p)
                act.activation(O[:, i, h * P:(h + 1) * P], acc[1][:, p % 2, 0:P], ACT.Copy)
                act.activation(ta[0][:, 0, 0:P], acc[1][:, p % 2, 0:P], ACT.Square, scale=(2 * HD) ** -0.5,
                               accum_out=ssC[:, i, h:h + 1]).then_inc(S["o_read"], 1)

            attention(pieces, lambda i: (i + 1) * P + META,
                      lambda i: [(0, i + 1, P), (i + 1, i + 2, META)], squares_of_out)
            act.wait_ge(S["c_var"], 1)
            link(act.activation(guC[:], vaC[:], ACT.Ln))
            act.activation(guC[:], guC[:], ACT.Exp, scale=-0.5).then_inc(S["c_guess"], 1)
            out_high(GAIN["attn_subln_2"])
            g = G["w_o"]
            sq0 = n.get("squares")
            for j in range(4):
                split(g.c0 + j + 2)
                gc = GAIN["mix_norm_post_2"] + KD + 2 * j
                post_unit(g, j, [F[:, 2 * j + m, META:] for m in range(2)], acc[(g.u0 + j) % 2],
                          [gain[:, gc + m:gc + m + 1] for m in range(2)], SEQ, sq0)
            n.add("squares", 4)
            root(SEQ)
            xg(PAIRS, PRE + 3 * KD, META, SEQ, D, waits=[1] * 4)
            ffn(3, META, SEQ, POST + 3 * KD)
            for q in range(4):
                act.wait_ge(S["y_turned"], q + 1)
                i, h = q // 2, q % 2
                act.activation(xrows[:, i, h * 512:(h + 1) * 512], acc[i][:, h, :], ACT.Copy).then_inc(S["y_rows"], 1)

        @block.vector
        def _(dve):
            n = Counts()

            def x_done():
                dve.wait_ge(S["x_ready"], n.get("x_ready"))

            def link(ins):
                ins.then_inc(S["dve_step"], 1)
                dve.wait_ge(S["dve_step"], n.add("dve_step"))

            def split(c, it=None, per=0):
                if c >= N_CHUNKS:
                    return
                dve.wait_ge(S["w_high"], at(c + 1, it, per))
                s = slice(0, SIZES[c])
                dve.tensor_tensor(wlo[c % 2][:, s], raw[c % 2][:, s], whi[c % 2][:, s].bitcast(F32), ALU.subtract)\
                    .then_inc(S["w_low"], 1)

            def unit_wait(g, j, it=None, per=0):
                sem_, value = unit_full(g, j)
                dve.wait_ge(sem_, at(value, it, per))

            def across(v, tiles):
                return v.unsqueeze(1).to_broadcast([v.shape[0], tiles, v.shape[1]])

            def add_squares(tiles, T, made="sq_made"):
                q = n.add("squares")
                if made:
                    dve.wait_ge(S[made], n.add(made))
                if q > 1:
                    dve.wait_ge(S["sq_read"], q - 1)
                for t in range(tiles):
                    ins = dve.tensor_tensor(sqsum[:, 0:T], sqsum[:, 0:T], sq[q % 2][:, t, 0:T], ALU.add)
                    if t < tiles - 1:
                        link(ins)
                ins.then_inc(S["sq_read"], 1)

            def xg(groups, gcol, T0, T, src=None, low=True, add=True):
                src = src or X
                for a, b in groups:
                    if low:
                        dve.wait_ge(S["xg_high"], n.add("xg_high"))
                        for k in range(a, b):
                            gc = gcol + k - groups[0][0]
                            ins = dve.scalar_tensor_tensor(XL[:, k, T0:T0 + T], src[:, k, T0:T0 + T],
                                                           gain[:, gc:gc + 1], XH[:, k, T0:T0 + T].bitcast(F32),
                                                           ALU.mult, ALU.subtract)
                        ins.then_inc(S["xg_ready"], 1)
                    if add:
                        add_squares(b - a, T)

            def variance(T):
                dve.wait_ge(S["norm_sum"], n.add("norm_sum"))
                dve.tensor_scalar(var[:, 0:T], normps[:, 0:T], EPS, None, ALU.add).then_inc(S["var_made"], 1)
                link(dve.memset(sqsum[:], 0.0))

            def refine(dst, T):
                dve.wait_ge(S["guess_made"], n.add("guess_made"))
                newton(dst[:, 0:T], guess[:, 0:T], var[:, 0:T], step[:, 0:T])

            def newton(dst, g_, v, s):
                link(dve.scalar_tensor_tensor(s, g_, -0.5, v, ALU.mult, ALU.mult))
                link(dve.tensor_tensor(s, s, g_, ALU.mult))
                link(dve.scalar_tensor_tensor(dst, s, 1.5, g_, ALU.add, ALU.mult))

            def scaled(g, j, dst, rows_, tiles, r, T, it=None, per=0, signal="dve_evac"):
                unit_wait(g, j, it, per)
                return dve.tensor_tensor(dst, acc[(g.u0 + j) % 2][0:rows_, 0:tiles, 0:T],
                                         across(r[0:rows_, 0:T], tiles), ALU.mult)

            def rope(u, rows_, tiles, cos, sin, dst, last=None):
                dve.wait_ge(S["rope_turned"], n.add("rope_turned"))
                x = ta[u % 2][0:rows_, 0:tiles, 0:SEQ]
                turned = sp[0][0:rows_, u % 2, 0:tiles * SEQ].rearrange("p (k t) -> p k t", k=tiles)
                dve.tensor_tensor(tb[0][0:rows_, 0:tiles, 0:SEQ], x, across(cos[0:rows_], tiles), ALU.mult)
                link(dve.tensor_tensor(tb[1][0:rows_, 0:tiles, 0:SEQ], turned, across(sin[0:rows_], tiles), ALU.mult))
                ins = dve.tensor_tensor(dst, tb[0][0:rows_, 0:tiles, 0:SEQ], tb[1][0:rows_, 0:tiles, 0:SEQ], ALU.add)
                if last:
                    ins.then_inc(S[last], 1)
                    dve.wait_ge(S[last], n.add(last))
                else:
                    link(ins)

            def rope_unit(g, j, rows_, tiles, r):
                scaled(g, j, ta[(g.u0 + j) % 2][0:rows_, 0:tiles, 0:SEQ], rows_, tiles, r, SEQ)\
                    .then_inc(S["dve_evac"], 1)
                dve.wait_ge(S["dve_evac"], g.r0 + j + 1)

            def residual(g, j, T):
                unit_wait(g, j)
                x = X[:, 2 * j:2 * j + 2, META:]
                dve.tensor_tensor(x, x, acc[(g.u0 + j) % 2][:, :, 0:T], ALU.add).then_inc(S["dve_evac"], 1)

            def mlp(layer, gcol):
                g = G[f"mlp_up{layer}"]

                def unit(j, it=None):
                    par = j % 2
                    unit_wait(g, j, it, 2)
                    dve.scalar_tensor_tensor(ta[par][:, :, 0:SEQ], acc[(g.u0 + j) % 2][:, :, 0:SEQ], 0.0,
                                             across(rstd[:, 0:SEQ], 2), ALU.max, ALU.mult).then_inc(S["dve_evac"], 1)
                    if j or it is not None:
                        split(g.c0 + j + 2, it, 2)
                    dve.wait_ge(S["hid_high"], at(hh0 + j + 1, it, 2))
                    h = 2 * j * SEQ
                    where = slice(h, h + 2 * SEQ) if it is None else ds(it * 4 * SEQ + h, 2 * SEQ)
                    pair = lambda v: v.rearrange("p (k t) -> p k t", k=2)
                    dve.tensor_tensor(pair(HL[:, where]), tb[par][:, :, 0:SEQ], pair(HH[:, where]).bitcast(F32),
                                      ALU.subtract).then_inc(S["hid_ready"], 1)

                hh0 = n.get("hid_high")
                variance(SEQ)
                split(g.c0 + 2)
                refine(rstd, SEQ)
                unit(0)
                unit(1)
                with dve.Fori(0, g.units // 2 - 2) as i:
                    for j in range(2, 4):
                        unit(j, i)
                for j in range(g.units - 2, g.units):
                    unit(j)
                n.add("hid_high", g.units)
                g = G[f"mlp_down{layer}"]
                sq0, xh0, sm0 = n.get("squares"), n.get("xg_high"), n.get("sq_made")

                def down_unit(j, it=None):
                    for q in range(2):
                        split(g.c0 + 2 * j + q + 2, it, 4)
                    sem_, value = unit_full(g, j)
                    dve.wait_ge(sem_, at(value, it, 4))
                    tile = (lambda v: v[:, j:j + 1, META:]) if it is None else \
                        (lambda v: v[:, ds(it * 2 + j, 1), META:])
                    dve.tensor_tensor(tile(X), tile(X), acc[(g.u0 + j) % 2][:, 0:1, 0:SEQ], ALU.add)\
                        .then_inc(S["dve_evac"], 1)
                    if gcol is not None:
                        dve.wait_ge(S["xg_high"], at(xh0 + j + 1, it, 2))
                        sc = gain[:, gcol + j:gcol + j + 1] if it is None else gain[:, ds(it * 2 + gcol + j, 1)]
                        dve.scalar_tensor_tensor(tile(XL), tile(X), sc, tile(XH).bitcast(F32), ALU.mult, ALU.subtract)\
                            .then_inc(S["xg_ready"], 1)
                    dve.wait_ge(S["sq_made"], at(sm0 + j + 1, it, 2))
                    if sq0 + j > 0:
                        dve.wait_ge(S["sq_read"], at(sq0 + j, it, 2))
                    dve.tensor_tensor(sqsum[:, 0:SEQ], sqsum[:, 0:SEQ], sq[(sq0 + j + 1) % 2][:, 0, 0:SEQ], ALU.add)\
                        .then_inc(S["sq_read"], 1)

                with dve.Fori(0, KD // 2 - 1) as i:
                    for j in range(2):
                        down_unit(j, i)
                for j in range(KD - 2, KD):
                    down_unit(j)
                n.add("squares", KD)
                n.add("sq_made", KD)
                if gcol is not None:
                    n.add("xg_high", KD)

            def post_norm(T0, T, signal="x_ready"):
                for q in range(4):
                    t = ta[q % 2][:, :, 0:T]
                    link(dve.tensor_tensor(t, F[:, 2 * q:2 * q + 2, T0:T0 + T], across(rstd[:, 0:T], 2), ALU.mult))
                    x = X[:, 2 * q:2 * q + 2, T0:T0 + T]
                    dve.tensor_tensor(x, x, t, ALU.add).then_inc(S[signal], 1)
                    n.add(signal)

            def ffn(i, T0, T, signal="x_ready"):
                g = G[f"ffn_up{i}"]

                def pair(j, it=None, first=False):
                    z, e, q, a = (v[:, :, 0:T] for v in (ta[0], tb[0], ta[1], tb[1]))
                    if first:
                        variance(T)
                        split(g.c0 + j + 2, it, 2)
                        refine(rstd, T)
                    unit_wait(g, j, it, 2)
                    dve.tensor_tensor(z, acc[(g.u0 + j) % 2][:, :, 0:T], across(rstd[:, 0:T], 2), ALU.mult)\
                        .then_inc(S["dve_evac"], 1)
                    if not first:
                        split(g.c0 + j + 2, it, 2)

                    dve.wait_ge(S["gate_silu"], at(ge0 + j // 2 + 1, it, 1))
                    dve.tensor_tensor(q, e, across(rstd[:, 0:T], 2), ALU.mult).then_inc(S["dve_step"], 1)
                    dve.wait_ge(S["dve_step"], at(st0 + j // 2 + 1, it, 1))
                    unit_wait(g, j + 1, it, 2)
                    dve.tensor_tensor(a, acc[(g.u0 + j + 1) % 2][:, :, 0:T], q, ALU.mult).then_inc(S["dve_evac"], 1)
                    split(g.c0 + j + 3, it, 2)
                    dve.wait_ge(S["hid_high"], at(hh0 + j // 2 + 1, it, 1))
                    h = j * T
                    where = slice(h, h + 2 * T) if it is None else ds(it * 2 * T + h, 2 * T)
                    two = lambda v: v.rearrange("p (k t) -> p k t", k=2)
                    dve.tensor_tensor(two(HL[:, where]), a, two(HH[:, where]).bitcast(F32), ALU.subtract)\
                        .then_inc(S["hid_ready"], 1)

                hh0, ge0, st0 = n.get("hid_high"), n.get("gate_silu"), None
                st0 = n.get("dve_step") + 4
                pair(0, first=True)
                assert n.get("dve_step") == st0
                with dve.Fori(0, g.units // 2 - 2) as it:
                    pair(2, it)
                pair(g.units - 2)
                n.add("dve_step", g.units // 2)
                n.add("hid_high", g.units // 2)
                n.add("gate_silu", g.units // 2)
                g = G[f"ffn_down{i}"]
                sq0 = n.get("squares")

                def unit(j, it=None):
                    split(g.c0 + j + 2, it, 2)
                    dve.wait_ge(S["act_evac"], at(g.r0 + j + 1, it, 2))
                    if sq0 + j > 0:
                        dve.wait_ge(S["sq_read"], at(sq0 + j, it, 2))
                    dve.tensor_tensor(sqsum[:, 0:T], sqsum[:, 0:T], sq[(sq0 + j + 1) % 2][:, 0, 0:T], ALU.add)\
                        .then_inc(S["sq_read"], 1)

                with dve.Fori(0, KD // 2 - 1) as it:
                    for j in range(2):
                        unit(j, it)
                for j in range(KD - 2, KD):
                    unit(j)
                n.add("squares", KD)
                variance(T)
                refine(rstd, T)
                post_norm(T0, T, signal)

            def attention(pieces, scale, keys, mask, outs, combine=None):
                s0, e0, o0 = n.get("s_full"), n.get("exp_done"), n.get("o_full")

                def scores(p):
                    i = pieces[p][0]
                    nk = keys(i)
                    s = Sm[p % 2][:, :, 0:nk]
                    dve.wait_ge(S["s_full"], s0 + p + 1)
                    if p >= 2:
                        dve.wait_ge(S["exp_done"], e0 + p - 1)
                    link(dve.scalar_tensor_tensor(s, sp[p % 2][:, :, 0:nk], scale, across(mask(i), 2), ALU.mult,
                                                  ALU.add))
                    dve.tensor_reduce(rowneg[:, p % 4], s, AX.X, ALU.max, negate=True).then_inc(S["s_read"], 1)

                N = len(pieces)
                for p in range(N):
                    scores(p)
                    if combine and p >= 1:
                        combine(p - 1, e0)
                    if outs and p >= 2:
                        outs(p - 2, *pieces[p - 2], o0)
                if combine:
                    combine(N - 1, e0)
                if outs:
                    outs(N - 2, *pieces[N - 2], o0)
                    outs(N - 1, *pieces[N - 1], o0)
                n.add("s_full", N)
                n.add("exp_done", N)
                n.add("o_full", N)

            def outs_of(heads):
                def outs(p, i, m, o0):
                    link(dve.reciprocal(rowinv[:, p % 4], rowsum[:, p % 4]))
                    dve.wait_ge(S["o_full"], o0 + p + 1)
                    dst = heads(O[:, i, :], m)
                    last = p == 15
                    src = acc[1][:, p % 2, 0:2 * HD].rearrange("p (c d) -> p c d", c=2)
                    dve.tensor_tensor(dst, src, rowinv[:, p % 4].unsqueeze(2).to_broadcast([P, 2, HD]), ALU.mult)\
                        .then_inc(S["o_read"], 1)
                return outs

            def out_low(gcol=None):
                for i in range(2):
                    for half_ in range(2):
                        dve.wait_ge(S["oT_high"], n.add("oT_high"))
                        dst = (slice(None), slice(4 * half_, 4 * half_ + 4), slice(META + i * P, META + (i + 1) * P))
                        src = sp[i][:, half_, :].rearrange("p (k t) -> p k t", k=4)
                        if gcol is None:
                            ins = dve.tensor_tensor(XL[dst], src, XH[dst].bitcast(F32), ALU.subtract)
                        else:
                            ins = dve.scalar_tensor_tensor(XL[dst], src, gain[:, gcol:gcol + 1], XH[dst].bitcast(F32),
                                                           ALU.mult, ALU.subtract)
                        ins.then_inc(S["oT_ready"], 1)

            link(dve.memset(sqsum[:], 0.0))
            dve.wait_ge(S["vec_turned"], 1)
            for j, (a, k) in enumerate(((0, N_VEC_A), (N_VEC_A, N_VEC_B))):
                link(dve.tensor_copy(gain[:, a:a + k], sp[1][:, j, 0:k]))
            dve.tensor_copy(X[:, :, 0:META], sp[0][:, 0, 0:KD * META].rearrange("p (k t) -> p k t", k=KD))
            for i in range(2):
                for h in range(2):
                    dve.wait_ge(S["xrow_turned"], 2 * i + h + 1)
                    dve.tensor_copy(X[:, 4 * h:4 * h + 4, META + i * P:META + (i + 1) * P],
                                    acc[i][:, h, :].rearrange("p (k t) -> p k t", k=4)).then_inc(S["x_ready"], 1)
                    n.add("x_ready")
            post = GAIN["ffn_norm_post_2"]
            link(dve.tensor_scalar(gain[:, post:post + 4 * KD], gain[:, post:post + 4 * KD], 0.5, None, ALU.mult))
            pb, ps_, sub_ = GAIN["pool_b_2"], GAIN["pool_scale_2"], GAIN["attn_subln_2"]
            link(dve.tensor_tensor(gain[:, pb:pb + KD], gain[:, pb:pb + KD], gain[:, ps_:ps_ + KD], ALU.mult))
            link(dve.tensor_scalar(gain[:, sub_:sub_ + 1], gain[:, sub_:sub_ + 1], 1.0 - LAMBDA_INIT, None, ALU.mult))
            dve.wait_ge(S["pos_in"], 16)
            link(dve.tensor_copy(posf[:], posi[:]))
            dve.wait_ge(S["const_in"], 16)
            for r, col in enumerate((C_INVA, C_INVB)):
                t = turns[r]
                link(dve.tensor_scalar(ang[r][:], posf[:], cst[:, col:col + 1], None, ALU.mult))
                link(dve.tensor_scalar(t[:], ang[r][:], 1 / (2 * math.pi), ROUND, ALU.mult, ALU.add))
                link(dve.tensor_scalar(t[:], t[:], ROUND, None, ALU.subtract))
                for part in TURN_PARTS:
                    link(dve.scalar_tensor_tensor(ang[r][:], t[:], -part, ang[r][:], ALU.mult, ALU.add))
                dve.tensor_scalar(ang[r][:], ang[r][:], 3.1415925, -3.1415925, ALU.min, ALU.max)\
                    .then_inc(S["angle_ready"], 1)
            for r, (hf, cs) in enumerate(((half[0], cosA), (half[1], cosB))):
                dve.wait_ge(S["half_ready"], r + 1)
                link(dve.scalar_tensor_tensor(cs[:], hf[:], -2.0, hf[:], ALU.mult, ALU.mult))
                link(dve.tensor_scalar(cs[:], cs[:], 1.0, None, ALU.add))
            dve.wait_ge(S["lambda_in"], 64)
            for q in range(2):
                link(dve.tensor_tensor(lprod[:, q], lrow[:, 2 * q], lrow[:, 2 * q + 1], ALU.mult))
            dve.tensor_reduce(lam[:, 0:2], lprod[:], AX.X, ALU.add).then_inc(S["lam_ready"], 1)
            dve.wait_ge(S["lam_exp"], 1)
            link(dve.tensor_tensor(lam[:, 4:5], lam[:, 3:4], lam[:, 2:3], ALU.subtract))
            link(dve.tensor_scalar(lam[:, 5:6], lam[:, 4:5], LAMBDA_INIT, None, ALU.subtract))
            split(0)
            xg(PAIRS, GAIN["attn_norm"], META, SEQ)
            split(1)

            g = G["a_in"]
            variance(SEQ)
            split(g.c0 + 2)
            refine(rstd, SEQ)
            kinds = [(qiA[:, 0:2], 2), (qiA[:, 2:4], 2), (kiA[:].unsqueeze(1), 1)] + \
                    [(qA[:, 2 * j:2 * j + 2], 2) for j in range(4)] + [(kA[:], 2)]
            for j in range(9):
                if j == 8:
                    scaled(g, 8, vF[:, 0:2, 0:SEQ], P, 2, rstd, SEQ).then_inc(S["dve_evac"], 1)
                elif j == 2:
                    unit_wait(g, 2)
                    dve.scalar_tensor_tensor(wiF[0:IDX_HEADS, :], acc[(g.u0 + 2) % 2][0:IDX_HEADS, 1, 0:SEQ],
                                             IDX_SCALE, rstd[0:IDX_HEADS, 0:SEQ], ALU.mult, ALU.mult)\
                        .then_inc(S["wi_in"], 1)
                    rope_unit(g, 2, P, 1, rstd)
                else:
                    rope_unit(g, j, P, kinds[j][1], rstd)
                if j:
                    split(g.c0 + j + 2)
                    dst, tiles = kinds[j - 1]
                    rope(j - 1, P, tiles, cosA, sinA, dst, "q_ready" if j == 8 else None)
            for q in range(8):
                i, m = q // 4, q % 4
                nk = (i + 1) * P
                if q == 0:
                    dve.wait_ge(S["wi_turned"], 1)
                    dve.tensor_copy(wiA[:], sp[1][:, 0, 0:2 * IDX_HEADS].rearrange("p (i h) -> p i h", i=2))\
                        .then_inc(S["wi_ready"], 1)
                    dve.wait_ge(S["wi_ready"], 1)
                dve.wait_ge(S["idx_relu"], q + 1)
                for c in range(2):
                    add_to = cst[:, C_CHUNK + i * SEQ:C_CHUNK + i * SEQ + nk] if m == 0 and c == 0 else \
                        score[:, i, 0:nk]
                    ins = dve.scalar_tensor_tensor(score[:, i, 0:nk], Sm[q % 2][:, c, 0:nk],
                                                   wiA[:, i, 2 * m + c:2 * m + c + 1], add_to, ALU.mult, ALU.add)
                    if c == 0:
                        link(ins)
                ins.then_inc(S["idx_read"], 1)
                dve.wait_ge(S["idx_read"], q + 1)
            for i in range(2):
                s = score[:, i, 0:(i + 1) * P]
                for _ in range(TOPK // 8):
                    link(dve.max(top8[:], s))
                    link(dve.match_replace(s, top8[:], s, TAKEN))
                link(dve.tensor_scalar(hide[:, i, 0:(i + 1) * P], s, TAKEN / 2, NEG, ALU.is_gt, ALU.mult))
            pieces = [(i, m) for m in range(8) for i in range(2)]

            def beside(o, m):
                return o[:, 2 * m * HD:(2 * m + 2) * HD].rearrange("p (c d) -> p c d", c=2)

            def four_apart(o, m):
                eight = o[:, 512 * (m // 4):512 * (m // 4 + 1)].rearrange("p (c r d) -> p c r d", c=2, r=4)
                return eight[:, :, m % 4]

            attention(pieces, A_SCALE, lambda i: (i + 1) * P, lambda i: hide[:, i, 0:(i + 1) * P], outs_of(four_apart))
            out_low()
            for j in range(4):
                split(G["a_out"].c0 + j + 2)
                residual(G["a_out"], j, SEQ)
                dve.wait_ge(S["dve_evac"], G["a_out"].r0 + j + 1)
            xg(PAIRS, GAIN["mlp_norm"], META, SEQ)
            mlp(0, GAIN["attn_norm"] + KD)

            g = G["b_in"]
            variance(SEQ)
            split(g.c0 + 2)
            refine(rstd, SEQ)
            for j in range(2):
                scaled(g, j, F[:, 2 * j:2 * j + 2, 0:SEQ], P, 2, rstd, SEQ).then_inc(S["dve_evac"], 1)
                split(g.c0 + j + 3)
            unit_wait(g, 2)
            u = g.u0 + 2
            dve.tensor_tensor(F[:, 4, 0:SEQ], acc[u % 2][:, 0, 0:SEQ], rstd[:, 0:SEQ], ALU.mult)\
                .then_inc(S["x_ready"], 1)
            n.add("x_ready")
            dve.tensor_tensor(ta[u % 2][0:B_QK, 0, 0:SEQ], acc[u % 2][0:B_QK, 1, 0:SEQ], rstd[0:B_QK, 0:SEQ],
                              ALU.mult).then_inc(S["dve_evac"], 1)
            xg([(0, 2), (2, 3)], GAIN["b_q_norm"], META, SEQ, src=Flat(F, META))
            xg([(3, 5)], GAIN["b_kv_norm"], META, SEQ, src=Flat(F, META), add=False)
            rope(u, B_QK, 1, cosB, sinB, kB[0:B_QK, 0:1, :], "kr_ready")
            variance(SEQ)
            refine(rstd, SEQ)
            add_squares(2, SEQ)
            g = G["q_up"]
            for j in range(8):
                rope_unit(g, j, B_QK, 2, rstd)
                if j % 2 == 1:
                    split(g.c0 + j // 2 + 2)
                if j == 1:
                    variance(SEQ)
                    refine(rstd2, SEQ)
                if j:
                    rope(g.u0 + j - 1, B_QK, 2, cosB, sinB, qB[0:B_QK, 2 * j - 2:2 * j])
            rope(g.u0 + 7, B_QK, 2, cosB, sinB, qB[0:B_QK, 14:16], "q_ready")
            g = G["kv_up"]
            dve.wait_ge(S["kr_spread"], 1)
            for j in range(8):
                if j % 2 == 0:
                    h = 2 * j
                    unit_wait(g, j)
                    bank = acc[(g.u0 + j) % 2][0:B_NOPE].rearrange("p m (h t) -> p (m h) t", h=2)
                    dve.tensor_tensor(kB[0:B_NOPE, h:h + 4, :], bank, across(rstd2[0:B_NOPE, 0:SEQ], 4), ALU.mult)\
                        .then_inc(S["dve_evac"], 1)
                else:
                    m = j - 1
                    scaled(g, j, vF[:, m:m + 2, 0:SEQ], P, 2, rstd2, SEQ).then_inc(S["dve_evac"], 1)
                    split(g.c0 + j // 2 + 2)
            attention(pieces, B_SCALE, lambda i: (i + 1) * P,
                      lambda i: cst[:, C_CHUNK + i * SEQ:C_CHUNK + i * SEQ + (i + 1) * P], outs_of(beside))
            out_low()
            for j in range(4):
                split(G["b_out"].c0 + j + 2)
                residual(G["b_out"], j, SEQ)
                dve.wait_ge(S["dve_evac"], G["b_out"].r0 + j + 1)
            xg(PAIRS, GAIN["mlp_norm"] + KD, META, SEQ)
            mlp(1, None)
            variance(SEQ)
            refine(rstd, SEQ)

            def normed(dst, gcol, T0, T, k):
                return dve.scalar_tensor_tensor(dst, X[:, k, T0:T0 + T], gain[:, gcol + k:gcol + k + 1], rstd[:, 0:T],
                                                ALU.mult, ALU.mult)
            for k in range(KD):
                ins = normed(X[:, k, META:], GAIN["final_norm"], META, SEQ, k)
                if k % 2:
                    ins.then_inc(S["x_ready"], 1)
                    n.add("x_ready")

            PRE = GAIN["ffn_norm_pre_2"]
            x_done()
            xg(PAIRS, PRE, 0, T2)
            ffn(0, 0, T2)
            for buf in (hnP, win[0], win[1]):
                link(dve.memset(buf[:, :, 0:PAD], 0.0))
            for _ in range(4):
                add_squares(2, T2)
            variance(T2)
            refine(rstd, T2)
            for k in range(KD):
                ins = normed(hnP[:, k, PAD:], GAIN["mix_norm_pre_2"], 0, T2, k)
            link(ins)
            dve.wait_ge(S["window_in"], 16)
            src = hnP
            for lvl, w in enumerate(WINDOWS):
                dst = win[lvl % 2]
                link(dve.tensor_tensor(dst[:, 2 * lvl:, PAD:], src[:, 2 * lvl:, PAD:],
                                       src[:, 2 * lvl:, PAD - w // 2:PAD - w // 2 + T2], ALU.add))
                d = dfP[:, 2 * lvl:2 * lvl + 2, :]
                link(dve.tensor_tensor(d, dst[:, 2 * lvl:2 * lvl + 2, PAD:], across(winv[:, lvl], 2), ALU.mult))
                ins = dve.tensor_tensor(d, d, hnP[:, 2 * lvl:2 * lvl + 2, PAD:], ALU.subtract)
                src = dst
            ins.then_inc(S["pool_ready"], 1)
            dve.wait_ge(S["pool_ready"], 1)
            dve.wait_ge(S["xg_high"], n.add("xg_high"))
            flat = lambda v: v.rearrange("p k t -> p (k t)")
            dve.tensor_tensor(flat(XL[:]), flat(dfP[:]), flat(XH[:]).bitcast(F32), ALU.subtract)\
                .then_inc(S["xg_ready"], 1)
            g = G["pool"]
            for j in range(4):
                add_squares(2, T2)
            split(g.c0 + 2)
            variance(T2)
            refine(rstd, T2)
            post_norm(0, T2)
            for i, pre in ((1, PRE + KD), (2, PRE + 2 * KD)):
                x_done()
                xg(PAIRS, pre, 0, T2)
                ffn(i, 0, T2)
            x_done()
            xg(PAIRS, GAIN["mix_norm_pre_2"] + KD, 0, T2)
            g = G["qkv"]
            variance(T2)
            split(g.c0 + 2)
            refine(rstd, T2)
            for j in range(12):
                u = g.u0 + j
                unit_wait(g, j)
                m = 2 * (j % 4)
                if j < 4:
                    dst, src, r = qC[:, m:m + 2, :], acc[u % 2][:, :, META:T2], rstd[:, META:T2]
                else:
                    dst = (kC if j < 8 else vF)[:, m:m + 2, :]
                    src, r = acc[u % 2][:, :, 0:T2], rstd[:, 0:T2]
                dve.tensor_tensor(dst, src, across(r, 2), ALU.mult).then_inc(S["dve_evac"], 1)
                if j:
                    split(g.c0 + j + 2)
            pieces = [(i, h) for h in range(DIFF_HEADS) for i in range(2)]

            def difference(p, e0):
                i = pieces[p][0]
                nk = (i + 1) * P + META
                dve.wait_ge(S["exp_done"], e0 + p + 1)
                link(dve.reciprocal(rowinv[:, p % 4], rowsum[:, p % 4]))
                link(dve.tensor_tensor(rowinv[:, p % 4, 1:2], rowinv[:, p % 4, 1:2], lam[:, 5:6], ALU.mult))
                a, b = Pr[p % 2][:, 0, 0:nk], Pr[p % 2][:, 1, 0:nk]
                link(dve.tensor_scalar(b, b, rowinv[:, p % 4, 1:2], None, ALU.mult))
                dve.scalar_tensor_tensor(a, a, rowinv[:, p % 4, 0:1], b, ALU.mult, ALU.add)\
                    .then_inc(S["probs_ready"], 1)

            attention(pieces, DIFF_SCALE, lambda i: (i + 1) * P + META,
                      lambda i: cst[:, C_CAUSAL + i * T2:C_CAUSAL + i * T2 + (i + 1) * P + META], None, difference)
            dve.wait_ge(S["o_read"], 3 * len(pieces))
            dve.tensor_scalar(vaC[:], ssC[:], EPS, None, ALU.add).then_inc(S["c_var"], 1)
            dve.wait_ge(S["c_guess"], 1)
            newton(rsC[:], guC[:], vaC[:], stC[:])
            for i in range(2):
                o = O[:, i, :].rearrange("p (h d) -> p h d", d=P)
                ins = dve.tensor_tensor(o, o, rsC[:, i].unsqueeze(2).to_broadcast([P, DIFF_HEADS, P]), ALU.mult)
            ins.then_inc(S["o_all"], 1)
            out_low(GAIN["attn_subln_2"])
            g = G["w_o"]
            for j in range(4):
                split(g.c0 + j + 2)
                dve.wait_ge(S["act_evac"], g.r0 + j + 1)
                add_squares(2, SEQ, None)
            variance(SEQ)
            refine(rstd, SEQ)
            post_norm(META, SEQ)
            x_done()
            xg(PAIRS, PRE + 3 * KD, META, SEQ)
            ffn(3, META, SEQ, "y_ready")


_INS = ['x', 'positions', 'attn_norm', 'mlp_norm', 'a_w_in', 'a_w_out', 'b_w_in', 'b_q_norm', 'b_kv_norm',
        'b_w_q_up', 'b_w_kv_up', 'b_w_out', 'mlp_w_up', 'mlp_w_down', 'final_norm', 'meta_tokens_2',
        'ffn_norm_pre_2', 'ffn_norm_post_2', 'ffn_w1_2', 'ffn_w3_2', 'ffn_w2_2', 'mix_norm_pre_2',
        'mix_norm_post_2', 'pool_w_2', 'pool_b_2', 'pool_scale_2', 'attn_w_qkv_2', 'attn_w_o_2',
        'attn_lambda_q1_2', 'attn_lambda_k1_2', 'attn_lambda_q2_2', 'attn_lambda_k2_2', 'attn_subln_2']


def kernel(**inputs):
    import numpy as _np
    import concourse.bacc as _bacc
    from concourse import mybir as _mybir
    from concourse.bass_utils import run_bass_kernel_spmd as _run

    nc = _bacc.Bacc("TRN2", target_bir_lowering=False, num_devices=1)
    arrays, args = {}, {}
    for name in _INS:
        a = _np.ascontiguousarray(inputs[name])
        arrays[f"in_{name}_dram"] = a
        args[name] = nc.dram_tensor(f"in_{name}_dram", a.shape, _mybir.dt.from_np(a.dtype), kind="ExternalInput").ap()
    tables = []
    for name, a in zip(("constants", "window"), constants()):
        arrays[f"in_{name}_dram"] = a
        tables.append(nc.dram_tensor(f"in_{name}_dram", a.shape, F32, kind="ExternalInput").ap())
    out = nc.dram_tensor("out_0_dram", (1, SEQ, D), F32, kind="ExternalOutput").ap()
    two_blocks_kernel(nc, args, *tables, out)
    r = _run(nc, [arrays], core_ids=[0])
    return r.results[0]["out_0_dram"]
```

```python
from contextlib import ExitStack
import math

import numpy as np

import concourse.bass as bass
from concourse import mybir

F32 = mybir.dt.float32
F32R = mybir.dt.float32r
I32 = mybir.dt.int32
ACT = mybir.ActivationFunctionType
ALU = mybir.AluOpType
AX = mybir.AxisListType
ds = bass.ds

P = 128
D = 1024
KD = D // P
SEQ = 256
META = 16
T2 = SEQ + META
CHUNK = 64
TOPK = 64
EPS = 1e-6
THETA = 500000.0

A_HEADS, A_KV, HD = 16, 4, 64
A_ROT = HD // 4
IDX_HEADS = 8
IDX_SCALE = (IDX_HEADS ** -0.5) * (HD ** -0.5)
A_SCALE = HD ** -0.5
Q_COLS, KV_COLS, QI_COLS = A_HEADS * HD, A_KV * HD, IDX_HEADS * HD

B_HEADS, B_NOPE, B_ROPE, B_V = 16, 64, 32, 64
B_QK = B_NOPE + B_ROPE
B_QL, B_KVL = 384, 256
KQL, KKV = B_QL // P, B_KVL // P
B_SCALE = B_QK ** -0.5

D_FF = 4 * D
KF = D_FF // P
D_FF2 = 256 * ((8 * D // 3 + 255) // 256)
KF2 = D_FF2 // P
WINDOWS = (2, 4, 8, 16)
DIFF_HEADS = 8
DIFF_SCALE = HD ** -0.5
LAMBDA_INIT = 0.8 - 0.6 * math.exp(-0.3 * 1)

SLOT = KF2 * P
NEG = -1e30
TAKEN = -3e38
SINGLES = [(k, k + 1) for k in range(KD)]
PAIRS = [(k, k + 2) for k in range(0, KD, 2)]

C_ID = 0
C_INVA = C_ID + P
C_INVB = C_INVA + 1
C_RA = C_INVB + 1
C_RB = C_RA + P
C_CHUNK = C_RB + B_QK
C_CAUSAL = C_CHUNK + 2 * SEQ
C_ALL = C_CAUSAL + 2 * T2

VEC_A = [("attn_norm", 2 * KD), ("mlp_norm", 2 * KD), ("final_norm", KD),
         ("ffn_norm_pre_2", 4 * KD), ("ffn_norm_post_2", 4 * KD)]
VEC_B = [("mix_norm_pre_2", 2 * KD), ("mix_norm_post_2", 2 * KD), ("pool_b_2", KD), ("pool_scale_2", KD),
         ("b_q_norm", KQL), ("b_kv_norm", KKV), ("attn_subln_2", 1)]
GAIN = {}
_row = 0
for _name, _rows in VEC_A + VEC_B:
    GAIN[_name] = _row
    _row += _rows
N_VEC_A = sum(r for _, r in VEC_A)
N_VEC_B = sum(r for _, r in VEC_B)

TURN_PARTS = []
_rest = 2 * math.pi
for _bits in (5, 13, 21):
    _part = math.floor(_rest * 2 ** _bits) / 2 ** _bits
    TURN_PARTS.append(_part)
    _rest -= _part
TURN_PARTS.append(_rest)
ROUND = 1.5 * 2 ** 23


def constants():
    c = np.zeros((P, C_ALL), np.float32)
    c[:, C_ID:C_ID + P] = np.eye(P)
    for head in (0, HD):
        for d in range(A_ROT // 2):
            c[head + A_ROT // 2 + d, C_RA + head + d] = -1
            c[head + d, C_RA + head + A_ROT // 2 + d] = 1
    for d in range(B_ROPE // 2):
        c[B_NOPE + B_ROPE // 2 + d, C_RB + B_NOPE + d] = -1
        c[B_NOPE + d, C_RB + B_NOPE + B_ROPE // 2 + d] = 1
    inv_a = np.float32(THETA) ** (-np.arange(0, A_ROT, 2, dtype=np.float32) / A_ROT)
    inv_b = np.float32(THETA) ** (-np.arange(0, B_ROPE, 2, dtype=np.float32) / B_ROPE)
    for head in (0, HD):
        c[head:head + A_ROT, C_INVA] = np.tile(inv_a, 2)
    c[B_NOPE:B_QK, C_INVB] = np.tile(inv_b, 2)
    key = np.arange(T2)[None]
    for i in range(2):
        row = (i * P + np.arange(P))[:, None]
        c[:, C_CHUNK + i * SEQ:C_CHUNK + (i + 1) * SEQ] = np.where(key[:, :SEQ] < (row // CHUNK + 1) * CHUNK, 0, NEG)
        c[:, C_CAUSAL + i * T2:C_CAUSAL + (i + 1) * T2] = np.where(key <= row + META, 0, NEG)
    t = np.arange(T2)
    window = np.stack([1.0 / np.minimum(t + 1, w) for w in WINDOWS]).astype(np.float32)
    return c, window


def at(n, it, per):
    return n if it is None else it * per + n


class Flat:

    def __init__(self, tensor, shift):
        self.tensor, self.shift = tensor, shift

    def __getitem__(self, key):
        p, k, t = key
        return self.tensor[p, k, t.start - self.shift:t.stop - self.shift]


class Counts:

    def __init__(self):
        self.n = {}

    def add(self, name, k=1):
        self.n[name] = self.n.get(name, 0) + k
        return self.n[name]

    def get(self, name):
        return self.n.get(name, 0)


class Gemm:

    def __init__(self, name, sizes, units, reader="dve_evac", dmas=None):
        self.name, self.sizes, self.units, self.reader = name, sizes, units, reader
        self.dmas = dmas or [1] * len(sizes)


def plan():
    def mlp(i):
        return [Gemm(f"mlp_up{i}", [KD * 256] * (KF // 2), KF // 2), Gemm(f"mlp_down{i}", [16 * P] * (KD * 2), KD)]

    def ffn(i):
        return [Gemm(f"ffn_up{i}", [KD * 256] * KF2, KF2), Gemm(f"ffn_down{i}", [KF2 * P] * KD, KD, "act_evac")]

    gemms = [
        Gemm("a_in", [KD * 256] * 2 + [KD * 136] + [KD * 256] * 6, 9, dmas=[1, 1, 3, 4, 4, 4, 4, 1, 1]),
        Gemm("a_out", [KD * 256] * 4, 4), *mlp(0),
        Gemm("b_in", [KD * 256] * 2 + [KD * 160], 3),
        Gemm("q_up", [KQL * 4 * B_QK] * 4, 8), Gemm("kv_up", [KKV * 4 * P] * 4, 8, dmas=[2 * KKV] * 4),
        Gemm("b_out", [KD * 256] * 4, 4), *mlp(1),
        *ffn(0), Gemm("pool", [8 * 256], 4, "act_evac"), *ffn(1),
        *ffn(2), Gemm("qkv", [KD * 256] * 12, 12), Gemm("w_o", [KD * 256] * 4, 4, "act_evac"), *ffn(3),
    ]
    chunk = unit = 0
    read = {"dve_evac": 0, "act_evac": 0}
    landed, total = [], [0, 0]
    for g in gemms:
        g.c0, g.u0, g.r0 = chunk, unit, read[g.reader]
        g.before = dict(read)
        chunk += len(g.sizes)
        unit += g.units
        read[g.reader] += g.units
        for k in g.dmas:
            total[len(landed) % 2] += 16 * k
            landed.append(total[len(landed) % 2])
    return {g.name: g for g in gemms}, [x for g in gemms for x in g.sizes], landed


def two_blocks_kernel(nc, A, consts, window, out):
    G, SIZES, LANDED = plan()
    N_CHUNKS = len(SIZES)
    ctx = ExitStack()
    with ctx:
        def sb(name, shape, dt=F32):
            return ctx.enter_context(nc.sbuf_tensor(name, shape, dt))

        def sem(name):
            return ctx.enter_context(nc.semaphore(name))

        cursor = [(nc.sbuf_base + 63) // 64 * 64]

        def place(name, shape, dt=F32, offset=None):
            size = 4 * int(np.prod(shape[1:]))
            if offset is None:
                offset = cursor[0]
                cursor[0] += (size + 31) // 32 * 32
                assert cursor[0] <= nc.sbuf_usable_end, name
            return nc.alloc_sbuf_tensor_at(name, shape, dt, offset=offset)

        raw = [place(f"w_raw{i}", [P, SLOT]) for i in range(2)]
        whi = [place(f"w_high{i}", [P, SLOT], F32R) for i in range(2)]
        wlo = [place(f"w_low{i}", [P, SLOT], F32R) for i in range(2)]
        X = place("x_state", [P, KD, T2])
        XH = place("xg_high", [P, KD, T2], F32R)
        XL = place("xg_low", [P, KD, T2], F32R)
        F = place("mixer_out", [P, KD, T2])
        cst = place("constants", [P, C_ALL])
        winv = place("window_inverse", [P, len(WINDOWS), T2])
        ones = place("ones", [P, P])
        eps = place("epsilon", [P, 1])
        gain = place("gains", [P, N_VEC_A + N_VEC_B])
        squares = place("squares", [P, KD, T2])
        sq = [squares[:, 2 * i:2 * i + 2] for i in range(2)]
        sqsum = place("square_sum", [P, T2])
        var = place("variance", [P, T2])
        guess = place("rstd_guess", [P, T2])
        step = place("rstd_step", [P, T2])
        rstd = place("rstd", [P, T2])
        ta = [place(f"evac_a{i}", [P, 2, T2]) for i in range(2)]
        tb = [place(f"evac_b{i}", [P, 2, T2]) for i in range(2)]
        cosA, sinA, cosB, sinB = (place(n, [P, SEQ]) for n in ("cos_a", "sin_a", "cos_b", "sin_b"))
        lam = place("lambda_cols", [P, 8])
        rowsum = place("row_sums", [P, 4, 2])
        rowneg = place("row_neg_max", [P, 4, 2])
        rowinv = place("row_inverse", [P, 4, 2])

        region = cursor[0]
        HH = place("hidden_high", [P, KF * SEQ], F32R)
        HL = place("hidden_low", [P, KF * SEQ], F32R)
        region_end = cursor[0]
        sub = [region]

        def alias(name, shape, dt=F32):
            t = place(name, shape, dt, offset=sub[0])
            sub[0] += 4 * int(np.prod(shape[1:]))
            assert sub[0] <= region_end, name
            return t

        Sm = [alias(f"scores{i}", [P, 2, T2]) for i in range(2)]
        Pr = [alias(f"probs{i}", [P, 2, T2]) for i in range(2)]
        PT = [alias(f"probs_T{i}", [P, 4, P]) for i in range(2)]
        O = alias("attn_out", [P, 2, D])
        per_layer = sub[0]
        qA = alias("a_q", [P, 8, SEQ])
        kA = alias("a_k", [P, 2, SEQ])
        vA = alias("a_v", [P, 2, KV_COLS])
        qiA = alias("a_qi", [P, 4, SEQ])
        kiA = alias("a_ki", [P, SEQ])
        wiF = alias("a_wi_features", [P, SEQ])
        wiA = alias("a_wi", [P, 2, IDX_HEADS])
        score = alias("a_score", [P, 2, SEQ])
        hide = alias("a_hide", [P, 2, SEQ])
        top8 = alias("a_top8", [P, 8])
        sub[0] = per_layer
        qB = alias("b_q", [P, B_HEADS, SEQ])
        kB = alias("b_k", [P, B_HEADS, SEQ])
        vB = alias("b_v", [P, 2, D])
        sub[0] = per_layer
        qC = alias("c_q", [P, DIFF_HEADS, SEQ])
        kC = alias("c_k", [P, DIFF_HEADS, T2])
        vC = alias("c_v", [P, 3, D])
        ssC = alias("c_square_sums", [P, 2, DIFF_HEADS])
        vaC = alias("c_variance", [P, 2, DIFF_HEADS])
        guC = alias("c_guess", [P, 2, DIFF_HEADS])
        stC = alias("c_step", [P, 2, DIFF_HEADS])
        rsC = alias("c_rstd", [P, 2, DIFF_HEADS])
        sub[0] = region
        PAD = max(WINDOWS)
        hnP = alias("pool_in", [P, KD, PAD + T2])
        win = [alias(f"pool_sum{i}", [P, KD, PAD + T2]) for i in range(2)]
        dfP = alias("pool_diff", [P, KD, T2])
        sub[0] = region
        meta_rows = alias("meta_rows", [META, D])
        vec_rows = [alias("vector_rows_a", [N_VEC_A, P]), alias("vector_rows_b", [N_VEC_B, P])]
        posi = alias("positions_int", [P, SEQ], I32)
        posf = alias("positions_float", [P, SEQ])
        ang = [alias(f"angle{i}", [P, SEQ]) for i in range(2)]
        turns = [alias(f"turns{i}", [P, SEQ]) for i in range(2)]
        half = [alias(f"half_sine{i}", [P, SEQ]) for i in range(2)]
        lrow = alias("lambda_rows", [P, 4, HD])
        lprod = alias("lambda_products", [P, 2, HD])

        xrows = F[:].rearrange("p k t -> p (k t)")[:, 0:2 * D].rearrange("p (i d) -> p i d", i=2)
        vF = F
        ident = cst[:, C_ID:C_ID + P]
        rotA, rotB = cst[:, C_RA:C_RA + P], cst[0:B_QK, C_RB:C_RB + B_QK]

        acc = [ctx.enter_context(nc.psum_tensor(f"acc{i}", [P, 2, 512], F32)) for i in range(2)]
        sp = [ctx.enter_context(nc.psum_tensor(f"spare{i}", [P, 2, 512], F32)) for i in range(2)]
        normps = sp[1][:, 1]

        rstd2 = place("rstd_second", [P, T2])
        names = """x_in meta_in vec_in const_in window_in pos_in lambda_in w_landed0 w_landed1 w_high w_low w_used
            dve_evac act_evac part_full ones_set ident_in gain_ready xrow_turned vec_turned x_ready xg_high
            xg_ready sq_made sq_read norm_sum log_made guess_made dve_step act_step hid_high hid_ready
            gate_silu rope_turned kr_ready kr_spread angle_ready half_ready lam_ready lam_exp v_turned
            v_ready wi_in wi_turned wi_ready idx_full idx_relu idx_read s_full s_read exp_done probs_ready
            pt_full pt_ready o_full o_read o_all o_turned oT_high oT_ready q_ready c_var c_guess pool_ready
            y_ready y_turned y_rows out_done""".split()
        S = {n: sem(n) for n in names}
        block = ctx.enter_context(nc.Block())

        @block.sync
        def _(sp_):
            def load_chunk(c, src, it=None, per=0, parts=None):
                if c >= 2 or it is not None:
                    sp_.wait_ge(S["w_low"], at(c - 1, it, per))
                dst = raw[c % 2]
                if parts is None:
                    k, n = src.shape[1], src.shape[2]
                    sp_.dma_start(dst[:, 0:k * n].rearrange("p (k n) -> p k n", k=k), src)\
                        .then_inc(S[f"w_landed{c % 2}"], 16)
                else:
                    k = src.shape[1]
                    wide = sum(n for _, n in parts)
                    v = dst[:, 0:k * wide].rearrange("p (k n) -> p k n", k=k)
                    o = 0
                    for j, (col, n) in enumerate(parts):
                        sp_.dma_start(v[:, :, o:o + n], src[:, :, col:col + n])\
                            .then_inc(S[f"w_landed{c % 2}"], 16)
                        o += n

            def rows(w):
                return w.rearrange("(k p) n -> p k n", p=P)

            def straight(name, w, n):
                for j in range(len(G[name].sizes)):
                    load_chunk(G[name].c0 + j, rows(w)[:, :, j * n:(j + 1) * n])

            def mlp(layer):
                up, down = G[f"mlp_up{layer}"], G[f"mlp_down{layer}"]
                w = rows(A["mlp_w_up"][layer])
                with sp_.Fori(0, KF // 4) as i:
                    for j in range(2):
                        load_chunk(up.c0 + j, w[:, :, ds(i * 512 + j * 256, 256)], i, 2)
                w = rows(A["mlp_w_down"][layer])
                with sp_.Fori(0, KD // 2) as i:
                    for j in range(4):
                        k0 = 16 * (j % 2)
                        load_chunk(down.c0 + j, w[:, k0:k0 + 16, ds(i * 2 * P + (j // 2) * P, P)], i, 4)

            def ffn(n):
                up, down = G[f"ffn_up{n}"], G[f"ffn_down{n}"]
                w = [rows(A[name][n // 2, n % 2]) for name in ("ffn_w1_2", "ffn_w3_2")]
                with sp_.Fori(0, KF2 // 2) as i:
                    for j in range(2):
                        load_chunk(up.c0 + j, w[j][:, :, ds(i * 256, 256)], i, 2)
                w = rows(A["ffn_w2_2"][n // 2, n % 2])
                with sp_.Fori(0, KD // 2) as i:
                    for j in range(2):
                        load_chunk(down.c0 + j, w[:, :, ds(i * 2 * P + j * P, P)], i, 2)

            for i in range(2):
                sp_.dma_start(xrows[:, i], A["x"][0, i * P:(i + 1) * P, :]).then_inc(S["x_in"], 16)
            w = rows(A["a_w_in"][0])
            c, qi0 = G["a_in"].c0, Q_COLS + 2 * KV_COLS
            ki0 = qi0 + QI_COLS
            for j in range(2):
                load_chunk(c + j, w[:, :, qi0 + 256 * j:qi0 + 256 * (j + 1)])
            load_chunk(c + 2, w, parts=[(ki0, HD), (ki0, HD), (ki0 + HD, IDX_HEADS)])
            for j in range(4):
                h = 8 * (j // 2) + 2 * (j % 2)
                load_chunk(c + 3 + j, w, parts=[(x * HD, HD) for x in (h, h + 4, h + 1, h + 5)])
            load_chunk(c + 7, w[:, :, Q_COLS:Q_COLS + KV_COLS])
            load_chunk(c + 8, w[:, :, Q_COLS + KV_COLS:Q_COLS + 2 * KV_COLS])
            straight("a_out", A["a_w_out"][0], 256)
            mlp(0)
            w = rows(A["b_w_in"][0])
            for j, (a, b) in enumerate(((0, 256), (256, 512), (512, 672))):
                load_chunk(G["b_in"].c0 + j, w[:, :, a:b])
            straight("q_up", A["b_w_q_up"][0], 4 * B_QK)
            for j in range(4):
                c = G["kv_up"].c0 + j
                sp_.wait_ge(S["w_low"], c - 1)
                src = rows(A["b_w_kv_up"][0])[:, :, j * 4 * P:(j + 1) * 4 * P]
                for k in range(KKV):
                    for t in range(2):
                        dst = raw[c % 2][:, (2 * k + t) * 2 * P:(2 * k + t + 1) * 2 * P]
                        sp_.dma_start(dst.rearrange("p (h d) -> p h d", h=4),
                                      src[:, k].rearrange("p (h t d) -> p h t d", h=4, t=2)[:, :, t])\
                            .then_inc(S[f"w_landed{c % 2}"], 16)
            straight("b_out", A["b_w_out"][0], 256)
            mlp(1)
            ffn(0)
            load_chunk(G["pool"].c0, A["pool_w_2"][0].rearrange("g (k p) n -> p (g k) n", p=P))
            ffn(1)
            ffn(2)
            straight("qkv", A["attn_w_qkv_2"][0], 256)
            straight("w_o", A["attn_w_o_2"][0], 256)
            ffn(3)
            for i in range(2):
                sp_.wait_ge(S["y_rows"], 2 * (i + 1))
                sp_.dma_start(out[0, i * P:(i + 1) * P, :], xrows[:, i]).then_inc(S["out_done"], 16)
            sp_.wait_ge(S["out_done"], 32)

        @block.gpsimd
        def _(pool):
            pool.memset(ones[:], 1.0)
            pool.memset(eps[:], EPS).then_inc(S["ones_set"], 1)
            pool.wait_ge(S["kr_ready"], 1)
            for h in range(1, B_HEADS):
                ins = pool.tensor_copy(kB[B_NOPE:B_QK, h, :], kB[B_NOPE:B_QK, 0, :])
            ins.then_inc(S["kr_spread"], 1)

        @block.tensor
        def _(pe):
            n = Counts()

            def begin(g, but=0):
                for name, value in g.before.items():
                    if value:
                        pe.wait_ge(S[name], value - (but if name == "dve_evac" else 0))

            def wait_unit(g, j, it=None, per=0):
                if j >= 2:
                    pe.wait_ge(S[g.reader], at(g.r0 + j - 1, it, per))

            def three(dst, high_w, low_w, high, low, first, last):
                pe.matmul(dst, high_w, high, start=first, stop=False)
                pe.matmul(dst, high_w, low, start=False, stop=False)
                return pe.matmul(dst, low_w, high, start=False, stop=last)

            def cols(c, a, b):
                return whi[c % 2][:, a:b], wlo[c % 2][:, a:b]

            def sum_squares(T, groups):
                pe.wait_ge(S["sq_read"], n.add("sq_read", groups))
                pe.matmul(normps[:, 0:T], ones[:], sqsum[:, 0:T], start=True, stop=True)\
                    .then_inc(S["norm_sum"], 1)

            def wide(g, j, T0, T, ready=None, it=None, per=0, tiles=None):
                c, u = g.c0 + j, g.u0 + j
                pe.wait_ge(S["w_low"], at(c + 1, it, per))
                wait_unit(g, j, it, per)
                for k in range(KD):
                    if ready is not None and ready[k] is not None:
                        pe.wait_ge(*ready[k])
                    for m in range(2):
                        if tiles is None:
                            w, rows_ = cols(c, k * 256 + m * P, k * 256 + (m + 1) * P), P
                        else:
                            w, rows_ = tiles(c, k, m)
                        ins = three(acc[u % 2][0:rows_, m, 0:T], *w, XH[:, k, T0:T0 + T], XL[:, k, T0:T0 + T],
                                    k == 0, k == KD - 1)
                ins.then_inc(S["w_used"], 1)

            def xg_waits(groups):
                waits = [None] * KD
                for a, b in groups:
                    waits[a] = (S["xg_ready"], n.add("xg_ready"))
                return waits

            def oT_waits():
                waits = [None] * KD
                waits[0] = (S["oT_ready"], n.add("oT_ready", 4))
                return waits

            def turn_rope(g, j, rows_, tiles, rot):
                u = g.u0 + j
                pe.wait_ge(S["dve_evac"], g.r0 + j + 1)
                pe.matmul(sp[0][0:rows_, u % 2, 0:tiles * SEQ], rot, ta[u % 2][0:rows_, 0:tiles, 0:SEQ],
                          start=True, stop=True).then_inc(S["rope_turned"], 1)

            def down(g, T, K, chunks):
                kc = K // chunks

                def unit(j, it=None):
                    u = g.u0 + j
                    wait_unit(g, j, it, 2)
                    opening = it is None and j == 0
                    for q in range(chunks):
                        c = g.c0 + j * chunks + q
                        pe.wait_ge(S["w_low"], at(c + 1, it, 2 * chunks))
                        for k in range(kc):
                            h = (q * kc + k) * T
                            if opening and q * kc + k == K - 2:
                                pe.wait_ge(S["hid_ready"], n.get("hid_ready"))
                            ins = three(acc[u % 2][:, 0, 0:T], *cols(c, k * P, (k + 1) * P), HH[:, h:h + T],
                                        HL[:, h:h + T], q == 0 and k == 0, q == chunks - 1 and k == kc - 1)
                        ins.then_inc(S["w_used"], 1)

                begin(g, but=1)
                pe.wait_ge(S["hid_ready"], n.get("hid_ready") - 1)
                unit(0)
                begin(g)
                unit(1)
                with pe.Fori(0, KD // 2 - 1) as i:
                    for j in range(2, 4):
                        unit(j, i)

            def up(g, T0, T, groups, outputs):
                begin(g)
                wide(g, 0, T0, T, xg_waits(groups))
                sum_squares(T, 1)
                wide(g, 1, T0, T)
                with pe.Fori(0, g.units // 2 - 1) as i:
                    for j in range(2, 4):
                        wide(g, j, T0, T, it=i, per=2)
                n.add("hid_ready", outputs)

            def mlp(layer):
                up(G[f"mlp_up{layer}"], META, SEQ, PAIRS, KF // 2)
                down(G[f"mlp_down{layer}"], SEQ, KF, 2)

            def ffn(i, T0, T):
                up(G[f"ffn_up{i}"], T0, T, PAIRS, KF2 // 2)
                down(G[f"ffn_down{i}"], T, KF2, 1)
                sum_squares(T, KD)

            def turn_v(g, tiles, token_tiles, src=vF):
                pe.wait_ge(S["dve_evac"], g.r0 + g.units)
                done = n.get("v_ready")
                q = 0
                for t0, nt in token_tiles:
                    for first in range(0, tiles, 4):
                        if q >= 4:
                            pe.wait_ge(S["v_ready"], done + q - 3)
                        for m in range(first, min(first + 4, tiles)):
                            ins = pe.transpose(sp[(q // 2) % 2][0:nt, q % 2, (m - first) * P:(m - first + 1) * P],
                                               src[:, m, t0:t0 + nt], ident)
                        ins.then_inc(S["v_turned"], 1)
                        q += 1
                pe.wait_ge(S["v_ready"], n.add("v_ready", q))

            def attention(pieces, scores, prob_tiles, values, probs_by):
                s0, t0, o0 = n.get("s_read"), n.get("pt_ready"), n.get("o_read")

                def make_scores(p):
                    if p >= 2:
                        pe.wait_ge(S["s_read"], s0 + p - 1)
                    for c, (q, k) in enumerate(scores(*pieces[p])):
                        ins = pe.matmul(sp[p % 2][:, c, 0:k.shape[1]], q, k, start=True, stop=True)
                    ins.then_inc(S["s_full"], 1)

                def turn_probs(p):
                    pe.wait_ge(S[probs_by], n.add(probs_by))
                    if p >= 2:
                        pe.wait_ge(S["pt_ready"], t0 + p - 1)
                    for slot, (c, k0, nk) in enumerate(prob_tiles(pieces[p][0])):
                        ins = pe.transpose(acc[0][0:nk, p % 2, slot * P:(slot + 1) * P], Pr[p % 2][:, c, k0:k0 + nk],
                                           ident)
                    ins.then_inc(S["pt_full"], 1)

                def make_out(p):
                    pe.wait_ge(S["pt_ready"], t0 + p + 1)
                    if p >= 2:
                        pe.wait_ge(S["o_read"], o0 + p - 1)
                    tiles = prob_tiles(pieces[p][0])
                    for slot, (c, k0, nk) in enumerate(tiles):
                        v = values(*pieces[p], c, k0 // P, nk)
                        w = v.shape[1]
                        first = slot == 0 or tiles[slot - 1][0] != c
                        last = slot == len(tiles) - 1 or tiles[slot + 1][0] != c
                        ins = pe.matmul(acc[1][:, p % 2, c * w:(c + 1) * w], PT[p % 2][0:nk, slot, :], v,
                                        start=first, stop=last)
                    ins.then_inc(S["o_full"], 1)

                N = len(pieces)
                make_scores(0)
                for p in range(N + 2):
                    if p + 1 < N:
                        make_scores(p + 1)
                    if 1 <= p <= N:
                        turn_probs(p - 1)
                    if p >= 2:
                        make_out(p - 2)
                n.add("s_read", N)
                n.add("pt_ready", N)
                n.add("o_read", N)

            def turn_out(signal, value):
                pe.wait_ge(S[signal], value)
                for i in range(2):
                    for half in range(2):
                        for k in range(4):
                            ins = pe.transpose(sp[i][:, half, k * P:(k + 1) * P],
                                               O[:, i, (4 * half + k) * P:(4 * half + k + 1) * P], ident)
                        ins.then_inc(S["o_turned"], 1)

            pe.wait_ge(S["ident_in"], 16)
            pe.wait_ge(S["x_in"], 32)
            for i in range(2):
                for halfk in range(2):
                    for k in range(4):
                        ins = pe.transpose(acc[i][:, halfk, k * P:(k + 1) * P],
                                           xrows[:, i, (4 * halfk + k) * P:(4 * halfk + k + 1) * P], ident)
                    ins.then_inc(S["xrow_turned"], 1)
            pe.wait_ge(S["vec_in"], 16 * (len(VEC_A) + len(VEC_B)))
            pe.wait_ge(S["meta_in"], 16)
            for j, rows_ in enumerate((N_VEC_A, N_VEC_B)):
                pe.transpose(sp[1][:, j, 0:rows_], vec_rows[j][:, :], ident[0:rows_, 0:rows_])
            for k in range(KD):
                ins = pe.transpose(sp[0][:, 0, k * META:(k + 1) * META], meta_rows[:, k * P:(k + 1) * P],
                                   ident[0:META, 0:META])
            ins.then_inc(S["vec_turned"], 1)

            g = G["a_in"]
            pe.wait_ge(S["const_in"], 16)
            pe.wait_ge(S["ones_set"], 1)
            wide(g, 0, META, SEQ, xg_waits(PAIRS))
            sum_squares(SEQ, 1)
            wide(g, 1, META, SEQ)
            turn_rope(g, 0, P, 2, rotA)

            def key_and_weights(c, k, m):
                a = k * 136 + m * P
                return cols(c, a, a + (P if m == 0 else IDX_HEADS)), (P if m == 0 else IDX_HEADS)

            wide(g, 2, META, SEQ, tiles=key_and_weights)
            turn_rope(g, 1, P, 2, rotA)
            for j in range(3, 7):
                wide(g, j, META, SEQ)
                turn_rope(g, j - 1, P, 1 if j == 3 else 2, rotA)
            wide(g, 7, META, SEQ)
            turn_rope(g, 6, P, 2, rotA)
            wide(g, 8, META, SEQ)
            turn_rope(g, 7, P, 2, rotA)

            pe.wait_ge(S["wi_in"], 1)
            for i in range(2):
                ins = pe.transpose(sp[1][:, 0, i * IDX_HEADS:(i + 1) * IDX_HEADS],
                                   wiF[0:IDX_HEADS, i * P:(i + 1) * P], ident[0:IDX_HEADS, 0:IDX_HEADS])
            ins.then_inc(S["wi_turned"], 1)
            pe.wait_ge(S["q_ready"], n.add("q_ready"))
            turn_v(g, 2, [(0, P), (P, P)])
            for q in range(8):
                i, m = q // 4, q % 4
                if q == 1:
                    pe.wait_ge(S["wi_ready"], 1)
                if q >= 2:
                    pe.wait_ge(S["idx_relu"], q - 1)
                for c in range(2):
                    r = slice(c * HD, (c + 1) * HD)
                    ins = pe.matmul(sp[q % 2][:, c, 0:(i + 1) * P], qiA[r, m, i * P:(i + 1) * P],
                                    kiA[r, 0:(i + 1) * P], start=True, stop=True)
                ins.then_inc(S["idx_full"], 1)
            pe.wait_ge(S["idx_relu"], 8)

            def halves(i):
                return [(c, k * P, P) for c in range(2) for k in range(i + 1)]

            begin(G["a_out"])
            attention([(i, m) for m in range(8) for i in range(2)],
                      lambda i, m: [(qA[c * HD:(c + 1) * HD, m, i * P:(i + 1) * P],
                                     kA[c * HD:(c + 1) * HD, m // 4, 0:(i + 1) * P]) for c in range(2)],
                      halves,
                      lambda i, m, c, kt, nk: vA[:, kt, (2 * (m // 4) + c) * HD:(2 * (m // 4) + c + 1) * HD],
                      "exp_done")
            turn_out("o_read", n.get("o_read"))
            g = G["a_out"]
            for j in range(4):
                wide(g, j, META, SEQ, oT_waits() if j == 0 else None)
            mlp(0)

            g = G["b_in"]
            begin(g)
            wide(g, 0, META, SEQ, xg_waits(SINGLES))
            sum_squares(SEQ, KD)
            wide(g, 1, META, SEQ)

            def latent_and_key(c, k, m):
                a = k * 160 + m * B_NOPE
                return cols(c, a, a + (P if m == 0 else B_QK)), (P if m == 0 else B_QK)

            wide(g, 2, META, SEQ, tiles=latent_and_key)
            turn_rope(g, 2, B_QK, 1, rotB)

            def latent_unit(g, j, last, tiles, k0, KK, rows_, it=None):
                u = g.u0 + j
                wait_unit(g, j)
                for t, (dst, weights) in enumerate(tiles(u)):
                    for k in range(KK):
                        ins = three(dst, *weights(k), XH[:, k0 + k, META:META + SEQ], XL[:, k0 + k, META:META + SEQ],
                                    k == 0, k == KK - 1)
                ins.then_inc(S["w_used" if last else "part_full"], 1)

            g = G["q_up"]
            begin(g)
            pe.wait_ge(S["xg_ready"], n.add("xg_ready", 2))
            sum_squares(SEQ, 1)
            for j in range(8):
                c = g.c0 + j // 2
                if j % 2 == 0:
                    pe.wait_ge(S["w_low"], c + 1)

                def heads(u, c=c, r=j % 2):
                    for m in range(2):
                        def weights(k, m=m):
                            a = k * 4 * B_QK + (2 * r + m) * B_QK
                            return cols(c, a, a + B_QK)
                        yield acc[u % 2][0:B_QK, m, 0:SEQ], weights
                latent_unit(g, j, j % 2 == 1, heads, 0, KQL, B_QK)
                if j == 0:
                    sum_squares(SEQ, 1)
                if j >= 1:
                    turn_rope(g, j - 1, B_QK, 2, rotB)
            turn_rope(g, 7, B_QK, 2, rotB)
            g = G["kv_up"]
            begin(g)
            pe.wait_ge(S["xg_ready"], n.add("xg_ready"))
            for j in range(8):
                c = g.c0 + j // 2
                if j % 2 == 0:
                    pe.wait_ge(S["w_low"], c + 1)

                def keys(u, c=c):
                    for h in range(4):
                        yield (acc[u % 2][0:B_NOPE, h // 2, (h % 2) * SEQ:(h % 2 + 1) * SEQ],
                               lambda k, h=h: cols(c, k * 4 * P + h * B_NOPE, k * 4 * P + (h + 1) * B_NOPE))

                def vals(u, c=c):
                    for m in range(2):
                        yield (acc[u % 2][:, m, 0:SEQ],
                               lambda k, m=m: cols(c, k * 4 * P + (m + 2) * P, k * 4 * P + (m + 3) * P))
                latent_unit(g, j, j % 2 == 1, keys if j % 2 == 0 else vals, KQL, KKV, P)
            pe.wait_ge(S["q_ready"], n.add("q_ready"))
            turn_v(g, 8, [(0, P), (P, P)])
            pe.wait_ge(S["kr_spread"], 1)
            begin(G["b_out"])
            attention([(i, m) for m in range(8) for i in range(2)],
                      lambda i, m: [(qB[0:B_QK, 2 * m + c, i * P:(i + 1) * P],
                                     kB[0:B_QK, 2 * m + c, 0:(i + 1) * P]) for c in range(2)],
                      halves,
                      lambda i, m, c, kt, nk: vB[:, kt, (2 * m + c) * B_V:(2 * m + c + 1) * B_V],
                      "exp_done")
            turn_out("o_read", n.get("o_read"))
            g = G["b_out"]
            for j in range(4):
                wide(g, j, META, SEQ, oT_waits() if j == 0 else None)
            mlp(1)
            sum_squares(SEQ, KD)

            ffn(0, 0, T2)
            sum_squares(T2, 1)
            g = G["pool"]
            begin(g)
            pe.wait_ge(S["w_low"], g.c0 + 1)
            for j in range(4):
                u = g.u0 + j
                pe.wait_ge(S["xg_ready"], n.add("xg_ready"))
                wait_unit(g, j)
                for m in range(2):
                    for k in range(2):
                        a = (2 * j + k) * 256 + m * P
                        ins = three(acc[u % 2][:, m, 0:T2], *cols(g.c0, a, a + P), XH[:, 2 * j + k, :],
                                    XL[:, 2 * j + k, :], k == 0, k == 1)
                ins.then_inc(S["w_used" if j == 3 else "part_full"], 1)
            sum_squares(T2, 4)
            ffn(1, 0, T2)
            ffn(2, 0, T2)
            g = G["qkv"]
            begin(g)
            wide(g, 0, 0, T2, xg_waits(PAIRS))
            sum_squares(T2, 1)
            for j in range(1, 12):
                wide(g, j, 0, T2)
            turn_v(g, 8, [(0, P), (P, P), (2 * P, META)])
            begin(G["w_o"])
            attention([(i, h) for h in range(DIFF_HEADS) for i in range(2)],
                      lambda i, h: [(qC[c * HD:(c + 1) * HD, h, i * P:(i + 1) * P],
                                     kC[c * HD:(c + 1) * HD, h, 0:(i + 1) * P + META]) for c in range(2)],
                      lambda i: [(0, k * P, P) for k in range(i + 1)] + [(0, (i + 1) * P, META)],
                      lambda i, h, c, kt, nk: vC[0:nk, kt, h * P:(h + 1) * P],
                      "probs_ready")
            turn_out("o_all", 1)
            g = G["w_o"]
            for j in range(4):
                wide(g, j, META, SEQ, oT_waits() if j == 0 else None)
            sum_squares(SEQ, 4)
            ffn(3, META, SEQ)
            pe.wait_ge(S["y_ready"], 4)
            for i in range(2):
                for halfk in range(2):
                    for k in range(4):
                        ins = pe.transpose(acc[i][:, halfk, k * P:(k + 1) * P],
                                           X[:, 4 * halfk + k, META + i * P:META + (i + 1) * P], ident)
                    ins.then_inc(S["y_turned"], 1)

        def unit_full(g, j):
            if g.name in ("q_up", "kv_up", "pool"):
                per_chunk = g.units // len(g.sizes)
                if j % per_chunk < per_chunk - 1:
                    done = {"q_up": 0, "kv_up": 4, "pool": 8}[g.name]
                    return S["part_full"], done + j // per_chunk * (per_chunk - 1) + j % per_chunk + 1
                return S["w_used"], g.c0 + j // per_chunk + 1
            chunks = len(g.sizes) // g.units
            return S["w_used"], g.c0 + (j + 1) * chunks

        @block.scalar
        def _(act):
            n = Counts()

            def link(ins):
                ins.then_inc(S["act_step"], 1)
                act.wait_ge(S["act_step"], n.add("act_step"))

            def split(c, it=None, per=0):
                if c >= N_CHUNKS:
                    return
                act.wait_ge(S[f"w_landed{c % 2}"], at(LANDED[c], it, 8 * per))
                if c >= 2:
                    act.wait_ge(S["w_used"], at(c - 1, it, per))
                act.activation(whi[c % 2][:, 0:SIZES[c]], raw[c % 2][:, 0:SIZES[c]], ACT.Copy).then_inc(S["w_high"], 1)

            def high_parts(a, b, gcol, T0, T, src):
                for k in range(a, b):
                    ins = act.activation(XH[:, k, T0:T0 + T], src[:, k, T0:T0 + T], ACT.Identity,
                                         scale=gain[:, gcol + k:gcol + k + 1])
                ins.then_inc(S["xg_high"], 1)

            def make_squares(a, b, T0, T, width, src):
                act.activation(squares[:, a:b, 0:T], src[:, a:b, T0:T0 + T], ACT.Square,
                               scale=width ** -0.5).then_inc(S["sq_made"], 1)

            def xg(gcol, T0, T, waits=(1, 1, 1, 1), high=True):
                for (a, b), k in zip(PAIRS, waits):
                    if k:
                        act.wait_ge(S["x_ready"], n.add("x_ready", k))
                    if high:
                        high_parts(a, b, gcol, T0, T, X)
                    make_squares(a, b, T0, T, D, X)
                n.add("squares")

            def latent_xg(groups, gcol, width):
                for a, b in groups:
                    high_parts(a, b, gcol, META, SEQ, Flat(F, META))
                    make_squares(a, b, 0, SEQ, width, F)
                n.add("squares")

            def residual(g, gcol, then):
                for j in range(4):
                    if j < 3:
                        split(g.c0 + j + 2)
                    act.wait_ge(S["dve_evac"], g.r0 + j + 1)
                    make_squares(2 * j, 2 * j + 2, META, SEQ, D, X)
                n.add("squares")
                act.wait_ge(S["w_used"], g.c0 + 4)
                for a, b in PAIRS:
                    high_parts(a, b, gcol, META, SEQ, X)
                split(then)

            def root(T):
                act.wait_ge(S["norm_sum"], n.add("norm_sum"))
                act.activation(guess[:, 0:T], normps[:, 0:T], ACT.Ln, bias=eps[:]).then_inc(S["log_made"], 1)
                act.wait_ge(S["log_made"], n.add("log_made"))
                act.activation(guess[:, 0:T], guess[:, 0:T], ACT.Exp, scale=-0.5).then_inc(S["guess_made"], 1)

            def mlp(layer, gcol):
                g = G[f"mlp_up{layer}"]

                def unit(j, it=None):
                    last = j == g.units - 1
                    if not last:
                        split(g.c0 + j + 2, it, 2)
                    par = j % 2
                    act.wait_ge(S["dve_evac"], at(g.r0 + j + 1, it, 2))
                    act.activation(tb[par][:, :, 0:SEQ], ta[par][:, :, 0:SEQ], ACT.Square).then_inc(S["act_step"], 1)
                    act.wait_ge(S["act_step"], at(step0 + j + 1, it, 2))
                    h = 2 * j * SEQ
                    dst = HH[:, h:h + 2 * SEQ] if it is None else HH[:, ds(it * 4 * SEQ + h, 2 * SEQ)]
                    act.activation(dst.rearrange("p (k t) -> p k t", k=2), tb[par][:, :, 0:SEQ], ACT.Copy)\
                        .then_inc(S["hid_high"], 1)
                    if last:
                        split(g.c0 + j + 2)

                root(SEQ)
                step0 = n.get("act_step")
                unit(0)
                unit(1)
                with act.Fori(0, g.units // 2 - 2) as i:
                    for j in range(2, 4):
                        unit(j, i)
                for j in range(g.units - 2, g.units):
                    unit(j)
                n.add("act_step", g.units)
                g = G[f"mlp_down{layer}"]
                sq0 = n.get("squares")

                def unit(j, it=None):
                    last = j == KD - 1
                    for q in range(1 if last else 2):
                        split(g.c0 + 2 * j + q + 2, it, 4)
                    act.wait_ge(S["sq_read"], at(sq0 + j - 1, it, 2))
                    act.wait_ge(S["dve_evac"], at(g.r0 + j + 1, it, 2))
                    if gcol is not None:
                        dst = XH[:, j, META:] if it is None else XH[:, ds(it * 2 + j, 1), META:]
                        src = X[:, j, META:] if it is None else X[:, ds(it * 2 + j, 1), META:]
                        sc = gain[:, gcol + j:gcol + j + 1] if it is None else gain[:, ds(it * 2 + gcol + j, 1)]
                        act.activation(dst, src, ACT.Identity, scale=sc).then_inc(S["xg_high"], 1)
                    par = (sq0 + j + 1) % 2
                    src = X[:, j:j + 1, META:] if it is None else X[:, ds(it * 2 + j, 1), META:]
                    act.activation(sq[par][:, 0:1, 0:SEQ], src, ACT.Square, scale=D ** -0.5).then_inc(S["sq_made"], 1)
                    if last and gcol is not None:
                        split(g.c0 + 2 * j + 3)

                with act.Fori(0, KD // 2 - 1) as i:
                    for j in range(2):
                        unit(j, i)
                for j in range(KD - 2, KD):
                    unit(j)
                n.add("squares", KD)

            def post_unit(g, j, dst, bank, gcols, T, sq0, it=None, per=0):
                sem_, value = unit_full(g, j)
                act.wait_ge(sem_, at(value, it, per))
                for m, (d, gc) in enumerate(zip(dst, gcols)):
                    act.activation(d, bank[:, m, 0:T], ACT.Identity, scale=gc)
                par = (sq0 + j + 1) % 2
                if sq0 + j + 1 > 2:
                    act.wait_ge(S["sq_read"], at(sq0 + j - 1, it, per))
                act.activation(sq[par][:, 0:len(dst), 0:T], bank[:, 0:len(dst), 0:T], ACT.Square,
                               scale=D ** -0.5).then_inc(S["act_evac"], 1)

            def ffn(i, T0, T):
                g = G[f"ffn_up{i}"]

                def pair(j, it=None, first=False, last=False):
                    if first:
                        root(T)
                        act.preload_act_table_set("silu_and_others")
                    split(g.c0 + j + 2, it, 2)
                    act.wait_ge(S["dve_evac"], at(g.r0 + j + 1, it, 2))
                    act.activation(tb[0][:, :, 0:T], ta[0][:, :, 0:T], ACT.Silu).then_inc(S["gate_silu"], 1)
                    if not last:
                        split(g.c0 + j + 3, it, 2)
                    act.wait_ge(S["dve_evac"], at(g.r0 + j + 2, it, 2))
                    h = j * T
                    dst = HH[:, h:h + 2 * T] if it is None else HH[:, ds(it * 2 * T + h, 2 * T)]
                    act.activation(dst.rearrange("p (k t) -> p k t", k=2), tb[1][:, :, 0:T], ACT.Copy)\
                        .then_inc(S["hid_high"], 1)
                    if last:
                        split(g.c0 + j + 3)

                pair(0, first=True)
                with act.Fori(0, g.units // 2 - 2) as it:
                    pair(2, it)
                pair(g.units - 2, last=True)
                act.preload_act_table_set("natural_log_exp_and_others")
                g = G[f"ffn_down{i}"]
                sq0 = n.get("squares")

                def unit(j, it=None):
                    if j < KD - 1:
                        split(g.c0 + j + 2, it, 2)
                    gcol = GAIN["ffn_norm_post_2"] + i * KD + j
                    dst = F[:, j, T0:T0 + T] if it is None else F[:, ds(it * 2 + j, 1), T0:T0 + T]
                    gc = gain[:, gcol:gcol + 1] if it is None else gain[:, ds(it * 2 + gcol, 1)]
                    post_unit(g, j, [dst], acc[(g.u0 + j) % 2], [gc], T, sq0, it, 2)

                with act.Fori(0, KD // 2 - 1) as it:
                    for j in range(2):
                        unit(j, it)
                for j in range(KD - 2, KD):
                    unit(j)
                n.add("squares", KD)
                root(T)

            def copy_v(dst):
                for q, (pieces, d) in enumerate(dst):
                    act.wait_ge(S["v_turned"], n.add("v_turned"))
                    act.activation(d, pieces, ACT.Copy).then_inc(S["v_ready"], 1)

            def attention(pieces, keys, slots, outs):
                s0, t0, o0 = n.get("s_read"), n.get("pt_full"), n.get("o_full")

                def exps(p):
                    act.wait_ge(S["s_read"], s0 + p + 1)
                    if p >= 2:
                        act.wait_ge(S["pt_full"], t0 + p - 1)
                    nk = keys(pieces[p][0])
                    for c in range(2):
                        ins = act.activation(Pr[p % 2][:, c, 0:nk], Sm[p % 2][:, c, 0:nk], ACT.Exp,
                                             bias=rowneg[:, p % 4, c:c + 1], accum_out=rowsum[:, p % 4, c:c + 1])
                    ins.then_inc(S["exp_done"], 1)

                def turned(p):
                    act.wait_ge(S["pt_full"], t0 + p + 1)
                    if p >= 2:
                        act.wait_ge(S["o_full"], o0 + p - 1)
                    for k0, k1, rows_ in slots(pieces[p][0]):
                        ins = act.activation(PT[p % 2][0:rows_, k0:k1, :], acc[0][0:rows_, p % 2, k0 * P:k1 * P]
                                             .rearrange("p (k t) -> p k t", t=P), ACT.Copy)
                    ins.then_inc(S["pt_ready"], 1)

                N = len(pieces)
                for p in range(N + 3):
                    if 2 <= p < N + 2:
                        turned(p - 2)
                    if p < N:
                        exps(p)
                    if outs and p >= 3:
                        outs(p - 3, *pieces[p - 3])
                n.add("s_read", N)
                n.add("pt_full", N)
                n.add("o_full", N)

            def out_high(gcol=None):
                for i in range(2):
                    for half_ in range(2):
                        act.wait_ge(S["o_turned"], n.add("o_turned"))
                        dst = XH[:, 4 * half_:4 * half_ + 4, META + i * P:META + (i + 1) * P]
                        src = sp[i][:, half_, :].rearrange("p (k t) -> p k t", k=4)
                        if gcol is None:
                            ins = act.activation(dst, src, ACT.Copy)
                        else:
                            ins = act.activation(dst, src, ACT.Identity, scale=gain[:, gcol:gcol + 1])
                        ins.then_inc(S["oT_high"], 1)

            act.dma_start(posi[:], A["positions"].rearrange("a t -> (a t)").partition_broadcast(P))\
                .then_inc(S["pos_in"], 16)
            act.dma_start(cst[:, 0:C_RA], consts[:, 0:C_RA]).then_inc(S["ident_in"], 16)
            for rows_, table in zip(vec_rows, (VEC_A, VEC_B)):
                a = 0
                for name, k in table:
                    src = A[name]
                    dims = len(src.shape)
                    flat = src if dims == 1 else src.rearrange(" ".join("abcd"[:dims]) + " -> (" +
                                                               " ".join("abcd"[:dims]) + ")")
                    act.dma_start(rows_[a:a + k, :], flat.rearrange("(k p) -> k p", p=P)).then_inc(S["vec_in"], 16)
                    a += k
            act.dma_start(meta_rows[:], A["meta_tokens_2"]).then_inc(S["meta_in"], 16)
            act.dma_start(cst[:, C_RA:], consts[:, C_RA:]).then_inc(S["const_in"], 16)
            for j, name in enumerate(("q1", "k1", "q2", "k2")):
                act.dma_start(lrow[:, j], A[f"attn_lambda_{name}_2"].rearrange("a d -> (a d)").partition_broadcast(P))\
                    .then_inc(S["lambda_in"], 16)
            act.dma_start(winv[:].rearrange("p w t -> p (w t)"), window.rearrange("w t -> (w t)")
                          .partition_broadcast(P)).then_inc(S["window_in"], 16)

            for r, (sn, hf) in enumerate(((sinA, half[0]), (sinB, half[1]))):
                act.wait_ge(S["angle_ready"], r + 1)
                act.activation(sn[:], ang[r][:], ACT.Sin)
                act.activation(hf[:], ang[r][:], ACT.Sin, scale=0.5).then_inc(S["half_ready"], 1)
            act.preload_act_table_set("natural_log_exp_and_others")
            split(0)
            act.wait_ge(S["gain_ready"], 2)
            xg(GAIN["attn_norm"], META, SEQ, (4, 0, 0, 0))
            split(1)
            act.wait_ge(S["lam_ready"], 1)
            act.activation(lam[:, 2:4], lam[:, 0:2], ACT.Exp).then_inc(S["lam_exp"], 1)

            g = G["a_in"]
            root(SEQ)
            for j in range(9):
                split(g.c0 + j + 2)
            copy_v([(sp[0][:, i, 0:KV_COLS], vA[:, i, :]) for i in range(2)])
            for q in range(8):
                act.wait_ge(S["idx_full"], q + 1)
                if q >= 2:
                    act.wait_ge(S["idx_read"], q - 1)
                nk = (q // 4 + 1) * P
                act.activation(Sm[q % 2][:, :, 0:nk], sp[q % 2][:, :, 0:nk], ACT.Relu).then_inc(S["idx_relu"], 1)
            pieces = [(i, m) for m in range(8) for i in range(2)]
            attention(pieces, lambda i: (i + 1) * P, lambda i: [(0, 2 * (i + 1), P)], None)
            out_high()
            residual(G["a_out"], GAIN["mlp_norm"], G["mlp_up0"].c0 + 1)
            mlp(0, GAIN["attn_norm"] + KD)

            g = G["b_in"]
            root(SEQ)
            split(g.c0 + 2)
            split(g.c0 + 3)
            split(g.c0 + 4)
            act.wait_ge(S["x_ready"], n.add("x_ready"))
            latent_xg([(0, 2), (2, 3)], GAIN["b_q_norm"], B_QL)
            latent_xg([(3, 5)], GAIN["b_kv_norm"] - KQL, B_KVL)
            root(SEQ)
            for j in range(4):
                split(G["q_up"].c0 + j + 2)
                if j == 0:
                    root(SEQ)
            for j in range(4):
                split(G["kv_up"].c0 + j + 2)
            copy_v([(sp[i][:, h, :], vB[:, i, h * 512:(h + 1) * 512]) for i in range(2) for h in range(2)])
            attention(pieces, lambda i: (i + 1) * P, lambda i: [(0, 2 * (i + 1), P)], None)
            out_high()
            residual(G["b_out"], GAIN["mlp_norm"] + KD, G["mlp_up1"].c0 + 1)
            mlp(1, None)
            root(SEQ)

            PRE = GAIN["ffn_norm_pre_2"]
            xg(PRE, 0, T2)
            split(G["ffn_up0"].c0 + 1)
            ffn(0, 0, T2)
            xg(None, 0, T2, high=False)
            split(G["ffn_up1"].c0)
            root(T2)
            for j in range(4):
                act.wait_ge(S["pool_ready"], j + 1)
                act.activation(XH[:, 2 * j:2 * j + 2, :], dfP[:, 2 * j:2 * j + 2, :], ACT.Copy)\
                    .then_inc(S["xg_high"], 1)
            g = G["pool"]
            sq0 = n.get("squares")
            for j in range(4):
                sem_, value = unit_full(g, j)
                act.wait_ge(sem_, value)
                bank = acc[(g.u0 + j) % 2]
                for m in range(2):
                    k = 2 * j + m
                    ins = act.activation(ta[j % 2][:, m, :], bank[:, m, 0:T2], ACT.Identity,
                                         scale=gain[:, GAIN["pool_scale_2"] + k:GAIN["pool_scale_2"] + k + 1],
                                         bias=gain[:, GAIN["pool_b_2"] + k:GAIN["pool_b_2"] + k + 1])
                ins.then_inc(S["act_evac"], 1)
                act.wait_ge(S["act_evac"], g.r0 + j + 1)
                for m in range(2):
                    k = 2 * j + m
                    gc = GAIN["mix_norm_post_2"] + k
                    act.activation(F[:, k, :], ta[j % 2][:, m, :], ACT.Identity, scale=gain[:, gc:gc + 1])
                par = n.add("squares") % 2
                act.wait_ge(S["sq_read"], n.get("squares") - 2)
                act.activation(sq[par][:], ta[j % 2][:], ACT.Square, scale=D ** -0.5).then_inc(S["sq_made"], 1)
            root(T2)
            xg(PRE + KD, 0, T2)
            split(G["ffn_up1"].c0 + 1)
            ffn(1, 0, T2)
            xg(PRE + 2 * KD, 0, T2)
            split(G["ffn_up2"].c0 + 1)
            ffn(2, 0, T2)
            xg(GAIN["mix_norm_pre_2"] + KD, 0, T2)
            g = G["qkv"]
            split(g.c0 + 1)
            root(T2)
            for j in range(12):
                split(g.c0 + j + 2)
            copy_v([(sp[i % 2][0:nt, h, :], vC[0:nt, i, h * 512:(h + 1) * 512])
                    for i, nt in enumerate((P, P, META)) for h in range(2)])
            pieces = [(i, h) for h in range(DIFF_HEADS) for i in range(2)]

            def squares_of_out(p, i, h):
                act.wait_ge(S["o_full"], n.get("o_full") + p + 1)
                if p:
                    act.wait_ge(S["o_read"], 2 * len(pieces) + p)
                act.activation(O[:, i, h * P:(h + 1) * P], acc[1][:, p % 2, 0:P], ACT.Copy)
                act.activation(ta[0][:, 0, 0:P], acc[1][:, p % 2, 0:P], ACT.Square, scale=(2 * HD) ** -0.5,
                               accum_out=ssC[:, i, h:h + 1]).then_inc(S["o_read"], 1)

            attention(pieces, lambda i: (i + 1) * P + META,
                      lambda i: [(0, i + 1, P), (i + 1, i + 2, META)], squares_of_out)
            act.wait_ge(S["c_var"], 1)
            link(act.activation(guC[:], vaC[:], ACT.Ln))
            act.activation(guC[:], guC[:], ACT.Exp, scale=-0.5).then_inc(S["c_guess"], 1)
            out_high(GAIN["attn_subln_2"])
            g = G["w_o"]
            sq0 = n.get("squares")
            for j in range(4):
                if j < 3:
                    split(g.c0 + j + 2)
                gc = GAIN["mix_norm_post_2"] + KD + 2 * j
                post_unit(g, j, [F[:, 2 * j + m, META:] for m in range(2)], acc[(g.u0 + j) % 2],
                          [gain[:, gc + m:gc + m + 1] for m in range(2)], SEQ, sq0)
            n.add("squares", 4)
            root(SEQ)
            xg(PRE + 3 * KD, META, SEQ)
            split(G["ffn_up3"].c0 + 1)
            ffn(3, META, SEQ)
            for q in range(4):
                act.wait_ge(S["y_turned"], q + 1)
                i, h = q // 2, q % 2
                act.activation(xrows[:, i, h * 512:(h + 1) * 512], acc[i][:, h, :], ACT.Copy).then_inc(S["y_rows"], 1)

        @block.vector
        def _(dve):
            n = Counts()

            def x_done():
                dve.wait_ge(S["x_ready"], n.get("x_ready"))

            def link(ins):
                ins.then_inc(S["dve_step"], 1)
                dve.wait_ge(S["dve_step"], n.add("dve_step"))

            def split(c, it=None, per=0):
                if c >= N_CHUNKS:
                    return
                dve.wait_ge(S["w_high"], at(c + 1, it, per))
                s = slice(0, SIZES[c])
                dve.tensor_tensor(wlo[c % 2][:, s], raw[c % 2][:, s], whi[c % 2][:, s].bitcast(F32), ALU.subtract)\
                    .then_inc(S["w_low"], 1)

            def unit_wait(g, j, it=None, per=0):
                sem_, value = unit_full(g, j)
                dve.wait_ge(sem_, at(value, it, per))

            def across(v, tiles):
                return v.unsqueeze(1).to_broadcast([v.shape[0], tiles, v.shape[1]])

            def add_squares(tiles, T, made="sq_made"):
                q = n.add("squares")
                if made:
                    dve.wait_ge(S[made], n.add(made))
                dve.wait_ge(S["sq_read"], q - 1)
                for t in range(tiles):
                    ins = dve.tensor_tensor(sqsum[:, 0:T], sqsum[:, 0:T], sq[q % 2][:, t, 0:T], ALU.add)
                    if t < tiles - 1:
                        link(ins)
                ins.then_inc(S["sq_read"], 1)

            def fold_squares(groups, tiles, T, first=0):
                dve.wait_ge(S["sq_made"], n.add("sq_made", groups))
                while tiles > 2:
                    up_ = tiles // 2
                    a, b = (squares[:, first + o:first + o + up_, 0:T] for o in (0, tiles - up_))
                    link(dve.tensor_tensor(a, a, b, ALU.add))
                    tiles -= up_
                a, b = (squares[:, first + o, 0:T] for o in (0, 1))
                dve.tensor_tensor(sqsum[:, 0:T], a, b, ALU.add).then_inc(S["sq_read"], 1)
                n.add("squares")

            def clear_sum():
                link(dve.memset(sqsum[:], 0.0))

            def low_parts(a, b, gcol, T0, T, src=None):
                src = src or X
                dve.wait_ge(S["xg_high"], n.add("xg_high"))
                for k in range(a, b):
                    gc = gcol + k
                    ins = dve.scalar_tensor_tensor(XL[:, k, T0:T0 + T], src[:, k, T0:T0 + T], gain[:, gc:gc + 1],
                                                   XH[:, k, T0:T0 + T].bitcast(F32), ALU.mult, ALU.subtract)
                ins.then_inc(S["xg_ready"], 1)

            def xg(gcol, T0, T, then):
                for a, b in PAIRS:
                    low_parts(a, b, gcol, T0, T)
                squares_after(then, T)

            def squares_after(then, T):
                fold_squares(4, KD, T)
                split(then)

            def variance(T):
                dve.wait_ge(S["log_made"], n.add("log_made"))
                link(dve.tensor_scalar(var[:, 0:T], normps[:, 0:T], EPS, None, ALU.add))

            def refine(dst, T):
                dve.wait_ge(S["guess_made"], n.add("guess_made"))
                newton(dst[:, 0:T], guess[:, 0:T], var[:, 0:T], step[:, 0:T])

            def newton(dst, g_, v, s):
                link(dve.scalar_tensor_tensor(s, g_, -0.5, v, ALU.mult, ALU.mult))
                link(dve.tensor_tensor(s, s, g_, ALU.mult))
                link(dve.scalar_tensor_tensor(dst, s, 1.5, g_, ALU.add, ALU.mult))

            def scaled(g, j, dst, rows_, tiles, r, T, it=None, per=0):
                unit_wait(g, j, it, per)
                return dve.tensor_tensor(dst, acc[(g.u0 + j) % 2][0:rows_, 0:tiles, 0:T],
                                         across(r[0:rows_, 0:T], tiles), ALU.mult)

            def rope(u, rows_, tiles, cos, sin, dst, last=None):
                dve.wait_ge(S["rope_turned"], n.add("rope_turned"))
                x = ta[u % 2][0:rows_, 0:tiles, 0:SEQ]
                turned = sp[0][0:rows_, u % 2, 0:tiles * SEQ].rearrange("p (k t) -> p k t", k=tiles)
                dve.tensor_tensor(tb[0][0:rows_, 0:tiles, 0:SEQ], x, across(cos[0:rows_], tiles), ALU.mult)
                link(dve.tensor_tensor(tb[1][0:rows_, 0:tiles, 0:SEQ], turned, across(sin[0:rows_], tiles), ALU.mult))
                ins = dve.tensor_tensor(dst, tb[0][0:rows_, 0:tiles, 0:SEQ], tb[1][0:rows_, 0:tiles, 0:SEQ], ALU.add)
                if last:
                    ins.then_inc(S[last], 1)
                    dve.wait_ge(S[last], n.add(last))
                else:
                    link(ins)

            def rope_unit(g, j, rows_, tiles, r):
                scaled(g, j, ta[(g.u0 + j) % 2][0:rows_, 0:tiles, 0:SEQ], rows_, tiles, r, SEQ)\
                    .then_inc(S["dve_evac"], 1)
                dve.wait_ge(S["dve_evac"], g.r0 + j + 1)

            def residual(g, gcol, then):
                for j in range(4):
                    if j < 3:
                        split(g.c0 + j + 2)
                    unit_wait(g, j)
                    x = X[:, 2 * j:2 * j + 2, META:]
                    dve.tensor_tensor(x, x, acc[(g.u0 + j) % 2][:, :, 0:SEQ], ALU.add).then_inc(S["dve_evac"], 1)
                dve.wait_ge(S["dve_evac"], g.r0 + 4)
                for a, b in PAIRS:
                    low_parts(a, b, gcol, META, SEQ)
                squares_after(then, SEQ)

            def mlp(layer, gcol):
                g = G[f"mlp_up{layer}"]

                def unit(j, it=None):
                    par = j % 2
                    unit_wait(g, j, it, 2)
                    dve.scalar_tensor_tensor(ta[par][:, :, 0:SEQ], acc[(g.u0 + j) % 2][:, :, 0:SEQ], 0.0,
                                             across(rstd[:, 0:SEQ], 2), ALU.max, ALU.mult).then_inc(S["dve_evac"], 1)
                    last = j == g.units - 1
                    if not last:
                        split(g.c0 + j + 2, it, 2)
                    dve.wait_ge(S["hid_high"], at(hh0 + j + 1, it, 2))
                    h = 2 * j * SEQ
                    where = slice(h, h + 2 * SEQ) if it is None else ds(it * 4 * SEQ + h, 2 * SEQ)
                    pair = lambda v: v.rearrange("p (k t) -> p k t", k=2)
                    dve.tensor_tensor(pair(HL[:, where]), tb[par][:, :, 0:SEQ], pair(HH[:, where]).bitcast(F32),
                                      ALU.subtract).then_inc(S["hid_ready"], 1)
                    if last:
                        split(g.c0 + j + 2)

                hh0 = n.get("hid_high")
                variance(SEQ)
                refine(rstd, SEQ)
                unit(0)
                unit(1)
                with dve.Fori(0, g.units // 2 - 2) as i:
                    for j in range(2, 4):
                        unit(j, i)
                for j in range(g.units - 2, g.units):
                    unit(j)
                n.add("hid_high", g.units)
                g = G[f"mlp_down{layer}"]
                sq0, xh0, sm0 = n.get("squares"), n.get("xg_high"), n.get("sq_made")

                def down_unit(j, it=None):
                    last = j == KD - 1
                    for q in range(1 if last else 2):
                        split(g.c0 + 2 * j + q + 2, it, 4)
                    sem_, value = unit_full(g, j)
                    dve.wait_ge(sem_, at(value, it, 4))
                    tile = (lambda v: v[:, j:j + 1, META:]) if it is None else \
                        (lambda v: v[:, ds(it * 2 + j, 1), META:])
                    dve.tensor_tensor(tile(X), tile(X), acc[(g.u0 + j) % 2][:, 0:1, 0:SEQ], ALU.add)\
                        .then_inc(S["dve_evac"], 1)
                    if gcol is not None:
                        dve.wait_ge(S["xg_high"], at(xh0 + j + 1, it, 2))
                        sc = gain[:, gcol + j:gcol + j + 1] if it is None else gain[:, ds(it * 2 + gcol + j, 1)]
                        dve.scalar_tensor_tensor(tile(XL), tile(X), sc, tile(XH).bitcast(F32), ALU.mult, ALU.subtract)\
                            .then_inc(S["xg_ready"], 1)
                    dve.wait_ge(S["sq_made"], at(sm0 + j + 1, it, 2))
                    dve.wait_ge(S["sq_read"], at(sq0 + j, it, 2))
                    dve.tensor_tensor(sqsum[:, 0:SEQ], sqsum[:, 0:SEQ], sq[(sq0 + j + 1) % 2][:, 0, 0:SEQ], ALU.add)\
                        .then_inc(S["sq_read"], 1)
                    if last and gcol is not None:
                        split(g.c0 + 2 * j + 3)

                clear_sum()
                with dve.Fori(0, KD // 2 - 1) as i:
                    for j in range(2):
                        down_unit(j, i)
                for j in range(KD - 2, KD):
                    down_unit(j)
                n.add("squares", KD)
                n.add("sq_made", KD)
                if gcol is not None:
                    n.add("xg_high", KD)

            def post_norm(T0, T, signal="x_ready", gcol=None):
                for q in range(4):
                    t = ta[q % 2][:, :, 0:T]
                    link(dve.tensor_tensor(t, F[:, 2 * q:2 * q + 2, T0:T0 + T], across(rstd[:, 0:T], 2), ALU.mult))
                    x = X[:, 2 * q:2 * q + 2, T0:T0 + T]
                    dve.tensor_tensor(x, x, t, ALU.add).then_inc(S[signal], 1)
                    n.add(signal)
                    if gcol is not None and q:
                        low_parts(2 * q - 2, 2 * q, gcol, T0, T)
                if gcol is not None:
                    x_done()
                    low_parts(KD - 2, KD, gcol, T0, T)

            def ffn(i, T0, T, signal="x_ready", gcol=None):
                g = G[f"ffn_up{i}"]

                def pair(j, it=None, first=False, last=False):
                    z, e, q, a = (v[:, :, 0:T] for v in (ta[0], tb[0], ta[1], tb[1]))
                    if first:
                        variance(T)
                        refine(rstd, T)
                    unit_wait(g, j, it, 2)
                    dve.tensor_tensor(z, acc[(g.u0 + j) % 2][:, :, 0:T], across(rstd[:, 0:T], 2), ALU.mult)\
                        .then_inc(S["dve_evac"], 1)
                    split(g.c0 + j + 2, it, 2)

                    dve.wait_ge(S["gate_silu"], at(ge0 + j // 2 + 1, it, 1))
                    dve.tensor_tensor(q, e, across(rstd[:, 0:T], 2), ALU.mult).then_inc(S["dve_step"], 1)
                    dve.wait_ge(S["dve_step"], at(st0 + j // 2 + 1, it, 1))
                    unit_wait(g, j + 1, it, 2)
                    dve.tensor_tensor(a, acc[(g.u0 + j + 1) % 2][:, :, 0:T], q, ALU.mult).then_inc(S["dve_evac"], 1)
                    if not last:
                        split(g.c0 + j + 3, it, 2)
                    dve.wait_ge(S["hid_high"], at(hh0 + j // 2 + 1, it, 1))
                    h = j * T
                    where = slice(h, h + 2 * T) if it is None else ds(it * 2 * T + h, 2 * T)
                    two = lambda v: v.rearrange("p (k t) -> p k t", k=2)
                    dve.tensor_tensor(two(HL[:, where]), a, two(HH[:, where]).bitcast(F32), ALU.subtract)\
                        .then_inc(S["hid_ready"], 1)
                    if last:
                        split(g.c0 + j + 3)

                hh0, ge0, st0 = n.get("hid_high"), n.get("gate_silu"), None
                st0 = n.get("dve_step") + 4
                pair(0, first=True)
                assert n.get("dve_step") == st0
                with dve.Fori(0, g.units // 2 - 2) as it:
                    pair(2, it)
                pair(g.units - 2, last=True)
                n.add("dve_step", g.units // 2)
                n.add("hid_high", g.units // 2)
                n.add("gate_silu", g.units // 2)
                g = G[f"ffn_down{i}"]
                sq0 = n.get("squares")

                def unit(j, it=None):
                    if j < KD - 1:
                        split(g.c0 + j + 2, it, 2)
                    dve.wait_ge(S["act_evac"], at(g.r0 + j + 1, it, 2))
                    dve.wait_ge(S["sq_read"], at(sq0 + j, it, 2))
                    dve.tensor_tensor(sqsum[:, 0:T], sqsum[:, 0:T], sq[(sq0 + j + 1) % 2][:, 0, 0:T], ALU.add)\
                        .then_inc(S["sq_read"], 1)

                clear_sum()
                with dve.Fori(0, KD // 2 - 1) as it:
                    for j in range(2):
                        unit(j, it)
                for j in range(KD - 2, KD):
                    unit(j)
                n.add("squares", KD)
                variance(T)
                refine(rstd, T)
                post_norm(T0, T, signal, gcol)

            def attention(pieces, scale, keys, mask, outs, combine=None):
                s0, e0, o0 = n.get("s_full"), n.get("exp_done"), n.get("o_full")

                def scores(p):
                    i = pieces[p][0]
                    nk = keys(i)
                    s = Sm[p % 2][:, :, 0:nk]
                    dve.wait_ge(S["s_full"], s0 + p + 1)
                    if p >= 2:
                        dve.wait_ge(S["exp_done"], e0 + p - 1)
                    link(dve.scalar_tensor_tensor(s, sp[p % 2][:, :, 0:nk], scale, across(mask(i), 2), ALU.mult,
                                                  ALU.add))
                    dve.tensor_reduce(rowneg[:, p % 4], s, AX.X, ALU.max, negate=True).then_inc(S["s_read"], 1)

                N = len(pieces)
                for p in range(N + 3):
                    if p < N:
                        scores(p)
                    if combine and 1 <= p <= N:
                        combine(p - 1, e0)
                    if outs and p >= 3:
                        outs(p - 3, *pieces[p - 3], o0)
                n.add("s_full", N)
                n.add("exp_done", N)
                n.add("o_full", N)

            def outs_of(heads):
                def outs(p, i, m, o0):
                    link(dve.reciprocal(rowinv[:, p % 4], rowsum[:, p % 4]))
                    dve.wait_ge(S["o_full"], o0 + p + 1)
                    dst = heads(O[:, i, :], m)
                    src = acc[1][:, p % 2, 0:2 * HD].rearrange("p (c d) -> p c d", c=2)
                    dve.tensor_tensor(dst, src, rowinv[:, p % 4].unsqueeze(2).to_broadcast([P, 2, HD]), ALU.mult)\
                        .then_inc(S["o_read"], 1)
                return outs

            def out_low(gcol=None):
                for i in range(2):
                    for half_ in range(2):
                        dve.wait_ge(S["oT_high"], n.add("oT_high"))
                        dst = (slice(None), slice(4 * half_, 4 * half_ + 4), slice(META + i * P, META + (i + 1) * P))
                        src = sp[i][:, half_, :].rearrange("p (k t) -> p k t", k=4)
                        if gcol is None:
                            ins = dve.tensor_tensor(XL[dst], src, XH[dst].bitcast(F32), ALU.subtract)
                        else:
                            ins = dve.scalar_tensor_tensor(XL[dst], src, gain[:, gcol:gcol + 1], XH[dst].bitcast(F32),
                                                           ALU.mult, ALU.subtract)
                        ins.then_inc(S["oT_ready"], 1)

            dve.wait_ge(S["pos_in"], 16)
            link(dve.tensor_copy(posf[:], posi[:]))
            dve.wait_ge(S["ident_in"], 16)
            for r, col in enumerate((C_INVA, C_INVB)):
                t = turns[r]
                link(dve.tensor_scalar(ang[r][:], posf[:], cst[:, col:col + 1], None, ALU.mult))
                link(dve.tensor_scalar(t[:], ang[r][:], 1 / (2 * math.pi), ROUND, ALU.mult, ALU.add))
                link(dve.tensor_scalar(t[:], t[:], ROUND, None, ALU.subtract))
                for part in TURN_PARTS:
                    link(dve.scalar_tensor_tensor(ang[r][:], t[:], -part, ang[r][:], ALU.mult, ALU.add))
                dve.tensor_scalar(ang[r][:], ang[r][:], 3.1415925, -3.1415925, ALU.min, ALU.max)\
                    .then_inc(S["angle_ready"], 1)
            for i in range(2):
                for h in range(2):
                    dve.wait_ge(S["xrow_turned"], 2 * i + h + 1)
                    dve.tensor_copy(X[:, 4 * h:4 * h + 4, META + i * P:META + (i + 1) * P],
                                    acc[i][:, h, :].rearrange("p (k t) -> p k t", k=4)).then_inc(S["x_ready"], 1)
                    n.add("x_ready")
            dve.wait_ge(S["vec_turned"], 1)
            for j, (a, k) in enumerate(((0, N_VEC_A), (N_VEC_A, N_VEC_B))):
                dve.tensor_copy(gain[:, a:a + k], sp[1][:, j, 0:k]).then_inc(S["gain_ready"], 1)
            dve.tensor_copy(X[:, :, 0:META], sp[0][:, 0, 0:KD * META].rearrange("p (k t) -> p k t", k=KD))
            split(0)
            x_done()
            dve.wait_ge(S["gain_ready"], 2)
            xg(GAIN["attn_norm"], META, SEQ, 1)
            for r, (hf, cs) in enumerate(((half[0], cosA), (half[1], cosB))):
                dve.wait_ge(S["half_ready"], r + 1)
                link(dve.scalar_tensor_tensor(cs[:], hf[:], -2.0, hf[:], ALU.mult, ALU.mult))
                link(dve.tensor_scalar(cs[:], cs[:], 1.0, None, ALU.add))
            dve.wait_ge(S["lambda_in"], 64)
            for q in range(2):
                link(dve.tensor_tensor(lprod[:, q], lrow[:, 2 * q], lrow[:, 2 * q + 1], ALU.mult))
            dve.tensor_reduce(lam[:, 0:2], lprod[:], AX.X, ALU.add).then_inc(S["lam_ready"], 1)
            post = GAIN["ffn_norm_post_2"]
            link(dve.tensor_scalar(gain[:, post:post + 4 * KD], gain[:, post:post + 4 * KD], 0.5, None, ALU.mult))
            pb, ps_, sub_ = GAIN["pool_b_2"], GAIN["pool_scale_2"], GAIN["attn_subln_2"]
            link(dve.tensor_tensor(gain[:, pb:pb + KD], gain[:, pb:pb + KD], gain[:, ps_:ps_ + KD], ALU.mult))
            link(dve.tensor_scalar(gain[:, sub_:sub_ + 1], gain[:, sub_:sub_ + 1], 1.0 - LAMBDA_INIT, None, ALU.mult))

            g = G["a_in"]
            variance(SEQ)
            dve.wait_ge(S["lam_exp"], 1)
            link(dve.tensor_tensor(lam[:, 4:5], lam[:, 3:4], lam[:, 2:3], ALU.subtract))
            link(dve.tensor_scalar(lam[:, 5:6], lam[:, 4:5], LAMBDA_INIT, None, ALU.subtract))
            refine(rstd, SEQ)
            kinds = [(qiA[:, 0:2], 2), (qiA[:, 2:4], 2), (kiA[:].unsqueeze(1), 1)] + \
                    [(qA[:, 2 * j:2 * j + 2], 2) for j in range(4)] + [(kA[:], 2)]
            for j in range(9):
                if j == 8:
                    scaled(g, 8, vF[:, 0:2, 0:SEQ], P, 2, rstd, SEQ).then_inc(S["dve_evac"], 1)
                elif j == 2:
                    unit_wait(g, 2)
                    dve.scalar_tensor_tensor(wiF[0:IDX_HEADS, :], acc[(g.u0 + 2) % 2][0:IDX_HEADS, 1, 0:SEQ],
                                             IDX_SCALE, rstd[0:IDX_HEADS, 0:SEQ], ALU.mult, ALU.mult)\
                        .then_inc(S["wi_in"], 1)
                    rope_unit(g, 2, P, 1, rstd)
                else:
                    rope_unit(g, j, P, kinds[j][1], rstd)
                split(g.c0 + j + 2)
                if j:
                    dst, tiles = kinds[j - 1]
                    rope(j - 1, P, tiles, cosA, sinA, dst, "q_ready" if j == 8 else None)
            for q in range(8):
                i, m = q // 4, q % 4
                nk = (i + 1) * P
                if q == 0:
                    dve.wait_ge(S["wi_turned"], 1)
                    dve.tensor_copy(wiA[:], sp[1][:, 0, 0:2 * IDX_HEADS].rearrange("p (i h) -> p i h", i=2))\
                        .then_inc(S["wi_ready"], 1)
                    dve.wait_ge(S["wi_ready"], 1)
                dve.wait_ge(S["idx_relu"], q + 1)
                for c in range(2):
                    add_to = cst[:, C_CHUNK + i * SEQ:C_CHUNK + i * SEQ + nk] if m == 0 and c == 0 else \
                        score[:, i, 0:nk]
                    ins = dve.scalar_tensor_tensor(score[:, i, 0:nk], Sm[q % 2][:, c, 0:nk],
                                                   wiA[:, i, 2 * m + c:2 * m + c + 1], add_to, ALU.mult, ALU.add)
                    if c == 0:
                        link(ins)
                ins.then_inc(S["idx_read"], 1)
                dve.wait_ge(S["idx_read"], q + 1)
            for i in range(2):
                s = score[:, i, 0:(i + 1) * P]
                for _ in range(TOPK // 8):
                    link(dve.max(top8[:], s))
                    link(dve.match_replace(s, top8[:], s, TAKEN))
                link(dve.tensor_scalar(hide[:, i, 0:(i + 1) * P], s, TAKEN / 2, NEG, ALU.is_gt, ALU.mult))
            pieces = [(i, m) for m in range(8) for i in range(2)]

            def beside(o, m):
                return o[:, 2 * m * HD:(2 * m + 2) * HD].rearrange("p (c d) -> p c d", c=2)

            def four_apart(o, m):
                eight = o[:, 512 * (m // 4):512 * (m // 4 + 1)].rearrange("p (c r d) -> p c r d", c=2, r=4)
                return eight[:, :, m % 4]

            attention(pieces, A_SCALE, lambda i: (i + 1) * P, lambda i: hide[:, i, 0:(i + 1) * P], outs_of(four_apart))
            out_low()
            residual(G["a_out"], GAIN["mlp_norm"], G["mlp_up0"].c0 + 1)
            mlp(0, GAIN["attn_norm"] + KD)

            g = G["b_in"]
            variance(SEQ)
            refine(rstd, SEQ)
            for j in range(2):
                scaled(g, j, F[:, 2 * j:2 * j + 2, 0:SEQ], P, 2, rstd, SEQ).then_inc(S["dve_evac"], 1)
                split(g.c0 + j + 2)
            split(g.c0 + 4)
            unit_wait(g, 2)
            u = g.u0 + 2
            dve.tensor_tensor(F[:, 4, 0:SEQ], acc[u % 2][:, 0, 0:SEQ], rstd[:, 0:SEQ], ALU.mult)\
                .then_inc(S["x_ready"], 1)
            n.add("x_ready")
            dve.tensor_tensor(ta[u % 2][0:B_QK, 0, 0:SEQ], acc[u % 2][0:B_QK, 1, 0:SEQ], rstd[0:B_QK, 0:SEQ],
                              ALU.mult).then_inc(S["dve_evac"], 1)
            latents = Flat(F, META)
            low_parts(0, 2, GAIN["b_q_norm"], META, SEQ, latents)
            low_parts(2, 3, GAIN["b_q_norm"], META, SEQ, latents)
            fold_squares(2, KQL, SEQ)
            low_parts(3, 5, GAIN["b_kv_norm"] - KQL, META, SEQ, latents)
            rope(u, B_QK, 1, cosB, sinB, kB[0:B_QK, 0:1, :], "kr_ready")
            variance(SEQ)
            refine(rstd, SEQ)
            fold_squares(1, KKV, SEQ, KQL)
            g = G["q_up"]
            for j in range(8):
                rope_unit(g, j, B_QK, 2, rstd)
                if j % 2 == 1:
                    split(g.c0 + j // 2 + 2)
                if j == 1:
                    variance(SEQ)
                    refine(rstd2, SEQ)
                if j:
                    rope(g.u0 + j - 1, B_QK, 2, cosB, sinB, qB[0:B_QK, 2 * j - 2:2 * j])
            rope(g.u0 + 7, B_QK, 2, cosB, sinB, qB[0:B_QK, 14:16], "q_ready")
            g = G["kv_up"]
            dve.wait_ge(S["kr_spread"], 1)
            for j in range(8):
                if j % 2 == 0:
                    h = 2 * j
                    unit_wait(g, j)
                    bank = acc[(g.u0 + j) % 2][0:B_NOPE].rearrange("p m (h t) -> p (m h) t", h=2)
                    dve.tensor_tensor(kB[0:B_NOPE, h:h + 4, :], bank, across(rstd2[0:B_NOPE, 0:SEQ], 4), ALU.mult)\
                        .then_inc(S["dve_evac"], 1)
                else:
                    m = j - 1
                    scaled(g, j, vF[:, m:m + 2, 0:SEQ], P, 2, rstd2, SEQ).then_inc(S["dve_evac"], 1)
                    split(g.c0 + j // 2 + 2)
            attention(pieces, B_SCALE, lambda i: (i + 1) * P,
                      lambda i: cst[:, C_CHUNK + i * SEQ:C_CHUNK + i * SEQ + (i + 1) * P], outs_of(beside))
            out_low()
            residual(G["b_out"], GAIN["mlp_norm"] + KD, G["mlp_up1"].c0 + 1)
            mlp(1, None)
            variance(SEQ)
            refine(rstd, SEQ)

            def normed(dst, gcol, T0, T, k):
                return dve.scalar_tensor_tensor(dst, X[:, k, T0:T0 + T], gain[:, gcol + k:gcol + k + 1], rstd[:, 0:T],
                                                ALU.mult, ALU.mult)
            for k in range(KD):
                ins = normed(X[:, k, META:], GAIN["final_norm"], META, SEQ, k)
                if k % 2:
                    ins.then_inc(S["x_ready"], 1)
                    n.add("x_ready")

            PRE = GAIN["ffn_norm_pre_2"]
            x_done()
            xg(PRE, 0, T2, G["ffn_up0"].c0 + 1)
            ffn(0, 0, T2)
            for buf in (hnP, win[0], win[1]):
                link(dve.memset(buf[:, :, 0:PAD], 0.0))
            fold_squares(4, KD, T2)
            variance(T2)
            split(G["ffn_up1"].c0)
            refine(rstd, T2)
            for k in range(KD):
                ins = normed(hnP[:, k, PAD:], GAIN["mix_norm_pre_2"], 0, T2, k)
            link(ins)
            dve.wait_ge(S["window_in"], 16)

            def pool_low(j):
                dve.wait_ge(S["xg_high"], n.add("xg_high"))
                t = (slice(None), slice(2 * j, 2 * j + 2))
                dve.tensor_tensor(XL[t], dfP[t], XH[t].bitcast(F32), ALU.subtract).then_inc(S["xg_ready"], 1)

            src = hnP
            for lvl, w in enumerate(WINDOWS):
                dst = win[lvl % 2]
                link(dve.tensor_tensor(dst[:, 2 * lvl:, PAD:], src[:, 2 * lvl:, PAD:],
                                       src[:, 2 * lvl:, PAD - w // 2:PAD - w // 2 + T2], ALU.add))
                s, x = (v[:, 2 * lvl:2 * lvl + 2, PAD:] for v in (dst, hnP))
                d = dfP[:, 2 * lvl:2 * lvl + 2, :]
                dve.scalar_tensor_tensor(d[:, :, w:], s[:, :, w:], 1 / w, x[:, :, w:], ALU.mult, ALU.subtract)
                link(dve.tensor_tensor(d[:, :, 0:w], s[:, :, 0:w], across(winv[:, lvl, 0:w], 2), ALU.mult))
                dve.tensor_tensor(d[:, :, 0:w], d[:, :, 0:w], x[:, :, 0:w], ALU.subtract).then_inc(S["pool_ready"], 1)
                if lvl:
                    pool_low(lvl - 1)
                src = dst
            dve.wait_ge(S["pool_ready"], 4)
            pool_low(3)
            clear_sum()
            for j in range(4):
                add_squares(2, T2)
            variance(T2)
            refine(rstd, T2)
            post_norm(0, T2, gcol=PRE + KD)
            squares_after(G["ffn_up1"].c0 + 1, T2)
            ffn(1, 0, T2, gcol=PRE + 2 * KD)
            squares_after(G["ffn_up2"].c0 + 1, T2)
            ffn(2, 0, T2, gcol=GAIN["mix_norm_pre_2"] + KD)
            g = G["qkv"]
            squares_after(g.c0 + 1, T2)
            variance(T2)
            refine(rstd, T2)
            for j in range(12):
                u = g.u0 + j
                unit_wait(g, j)
                m = 2 * (j % 4)
                if j < 4:
                    dst, src, r = qC[:, m:m + 2, :], acc[u % 2][:, :, META:T2], rstd[:, META:T2]
                else:
                    dst = (kC if j < 8 else vF)[:, m:m + 2, :]
                    src, r = acc[u % 2][:, :, 0:T2], rstd[:, 0:T2]
                dve.tensor_tensor(dst, src, across(r, 2), ALU.mult).then_inc(S["dve_evac"], 1)
                split(g.c0 + j + 2)
            pieces = [(i, h) for h in range(DIFF_HEADS) for i in range(2)]

            def difference(p, e0):
                i = pieces[p][0]
                nk = (i + 1) * P + META
                dve.wait_ge(S["exp_done"], e0 + p + 1)
                link(dve.reciprocal(rowinv[:, p % 4], rowsum[:, p % 4]))
                link(dve.tensor_tensor(rowinv[:, p % 4, 1:2], rowinv[:, p % 4, 1:2], lam[:, 5:6], ALU.mult))
                a, b = Pr[p % 2][:, 0, 0:nk], Pr[p % 2][:, 1, 0:nk]
                link(dve.tensor_scalar(b, b, rowinv[:, p % 4, 1:2], None, ALU.mult))
                dve.scalar_tensor_tensor(a, a, rowinv[:, p % 4, 0:1], b, ALU.mult, ALU.add)\
                    .then_inc(S["probs_ready"], 1)

            attention(pieces, DIFF_SCALE, lambda i: (i + 1) * P + META,
                      lambda i: cst[:, C_CAUSAL + i * T2:C_CAUSAL + i * T2 + (i + 1) * P + META], None, difference)
            dve.wait_ge(S["o_read"], 3 * len(pieces))
            dve.tensor_scalar(vaC[:], ssC[:], EPS, None, ALU.add).then_inc(S["c_var"], 1)
            dve.wait_ge(S["c_guess"], 1)
            newton(rsC[:], guC[:], vaC[:], stC[:])
            for i in range(2):
                o = O[:, i, :].rearrange("p (h d) -> p h d", d=P)
                ins = dve.tensor_tensor(o, o, rsC[:, i].unsqueeze(2).to_broadcast([P, DIFF_HEADS, P]), ALU.mult)
            ins.then_inc(S["o_all"], 1)
            out_low(GAIN["attn_subln_2"])
            g = G["w_o"]
            clear_sum()
            for j in range(4):
                if j < 3:
                    split(g.c0 + j + 2)
                dve.wait_ge(S["act_evac"], g.r0 + j + 1)
                add_squares(2, SEQ, None)
            variance(SEQ)
            refine(rstd, SEQ)
            post_norm(META, SEQ, gcol=PRE + 3 * KD)
            squares_after(G["ffn_up3"].c0 + 1, SEQ)
            ffn(3, META, SEQ, "y_ready")


_INS = ['x', 'positions', 'attn_norm', 'mlp_norm', 'a_w_in', 'a_w_out', 'b_w_in', 'b_q_norm', 'b_kv_norm',
        'b_w_q_up', 'b_w_kv_up', 'b_w_out', 'mlp_w_up', 'mlp_w_down', 'final_norm', 'meta_tokens_2',
        'ffn_norm_pre_2', 'ffn_norm_post_2', 'ffn_w1_2', 'ffn_w3_2', 'ffn_w2_2', 'mix_norm_pre_2',
        'mix_norm_post_2', 'pool_w_2', 'pool_b_2', 'pool_scale_2', 'attn_w_qkv_2', 'attn_w_o_2',
        'attn_lambda_q1_2', 'attn_lambda_k1_2', 'attn_lambda_q2_2', 'attn_lambda_k2_2', 'attn_subln_2']


def kernel(**inputs):
    import numpy as _np
    import concourse.bacc as _bacc
    from concourse import mybir as _mybir
    from concourse.bass_utils import run_bass_kernel_spmd as _run

    nc = _bacc.Bacc("TRN2", target_bir_lowering=False, num_devices=1)
    arrays, args = {}, {}
    for name in _INS:
        a = _np.ascontiguousarray(inputs[name])
        arrays[f"in_{name}_dram"] = a
        args[name] = nc.dram_tensor(f"in_{name}_dram", a.shape, _mybir.dt.from_np(a.dtype), kind="ExternalInput").ap()
    tables = []
    for name, a in zip(("constants", "window"), constants()):
        arrays[f"in_{name}_dram"] = a
        tables.append(nc.dram_tensor(f"in_{name}_dram", a.shape, F32, kind="ExternalInput").ap())
    out = nc.dram_tensor("out_0_dram", (1, SEQ, D), F32, kind="ExternalOutput").ap()
    two_blocks_kernel(nc, args, *tables, out)
    r = _run(nc, [arrays], core_ids=[0])
    return r.results[0]["out_0_dram"]
```
